# Optimizing a Trainium2 kernel written in Bass

```python
import jax, jax.numpy as jnp
from jax import lax
import numpy as np

D_MODEL = 2048
BATCH = 1
SEQ = 256
DEPTH = 1
DEC_BATCH = 8
DEC_SEQ = 16
PAST_LEN = 256

CHUNK = 64
N_HEADS = 16
HEAD_DIM = 64
ATTN_W = N_HEADS * HEAD_DIM
POOL_WINDOWS = (2, 4, 8, 16)
POOL_GROUPS = 4
POOL_W = 1024
POOL_GW = POOL_W // POOL_GROUPS
POOL_OUT_GW = D_MODEL // POOL_GROUPS
POOL_HIST = 15
D_FF = 4 * D_MODEL
Q_BLOCK = 128
EPS = 1e-6
SCALE = HEAD_DIM ** -0.5
OFF_Q = 0
OFF_K = OFF_Q + ATTN_W
OFF_V = OFF_K + ATTN_W
OFF_F = OFF_V + ATTN_W
OFF_U = OFF_F + N_HEADS
OFF_GA = OFF_U + POOL_W
OFF_GB = OFF_GA + D_MODEL
IN_W = OFF_GB + D_MODEL

kernel_name = "fox_pool_gated_streaming_encoder"

def rmsnorm(x, g):
    xf = x.astype(jnp.float32)
    y = xf * lax.rsqrt(jnp.mean(xf * xf, axis=-1, keepdims=True) + EPS)
    return (y * g.astype(jnp.float32)).astype(x.dtype)

def split_projection(h, w_in, b_f):
    B, T, _ = h.shape
    p = h @ w_in
    q = p[..., OFF_Q:OFF_K].reshape(B, T, N_HEADS, HEAD_DIM)
    k = p[..., OFF_K:OFF_V].reshape(B, T, N_HEADS, HEAD_DIM)
    v = p[..., OFF_V:OFF_F].reshape(B, T, N_HEADS, HEAD_DIM)
    logf = jax.nn.log_sigmoid(p[..., OFF_F:OFF_U].astype(jnp.float32) + b_f.astype(jnp.float32))
    u = p[..., OFF_U:OFF_GA]
    ga = p[..., OFF_GA:OFF_GB]
    gb = p[..., OFF_GB:IN_W]
    return q, k, v, logf, u, ga, gb

def forgetting_attend(q, k, v, cq, ck, qpos, kpos):
    s = jnp.einsum('bqhd,bkhd->bhqk', q, k).astype(jnp.float32) * SCALE
    bias = jnp.transpose(cq, (0, 2, 1))[..., :, None] - jnp.transpose(ck, (0, 2, 1))[..., None, :]
    mask = kpos[None, :] <= qpos[:, None]
    s = jnp.where(mask, s + bias, -jnp.inf)
    p = jax.nn.softmax(s, axis=-1)
    return jnp.einsum('bhqk,bkhd->bqhd', p.astype(v.dtype), v)

def fox_prompt(q, k, v, logf):
    B, T, H, dh = q.shape
    nb = T // Q_BLOCK
    c = jnp.cumsum(logf, axis=1)
    qb = jnp.transpose(q.reshape(B, nb, Q_BLOCK, H, dh), (1, 0, 2, 3, 4))
    cqb = jnp.transpose(c.reshape(B, nb, Q_BLOCK, H), (1, 0, 2, 3))
    posb = jnp.arange(T).reshape(nb, Q_BLOCK)
    kpos = jnp.arange(T)
    o = lax.map(lambda a: forgetting_attend(a[0], k, v, a[1], c, a[2], kpos), (qb, cqb, posb))
    return jnp.transpose(o, (1, 0, 2, 3, 4)).reshape(B, T, H * dh)

def fox_sample(q, k_all, v_all, logf_all, past):
    B, n, H, dh = q.shape
    c = jnp.cumsum(logf_all.astype(jnp.float32), axis=1)
    qpos = past + jnp.arange(n)
    kpos = jnp.arange(past + n)
    o = forgetting_attend(q, k_all, v_all, c[:, past:], c, qpos, kpos)
    return o.reshape(B, n, H * dh)

def multi_scale_pool(u_hist, u, pos):
    B, n, P = u.shape
    L = POOL_HIST
    ext = jnp.concatenate([u_hist.astype(u.dtype), u], axis=1).astype(jnp.float32)
    cs = jnp.concatenate([jnp.zeros((B, 1, P), jnp.float32), jnp.cumsum(ext, axis=1)], axis=1)
    outs = []
    for g, w in enumerate(POOL_WINDOWS):
        csg = cs[..., g * POOL_GW:(g + 1) * POOL_GW]
        tot = csg[:, L + 1:L + 1 + n] - csg[:, L + 1 - w:L + 1 - w + n]
        cnt = jnp.minimum(pos + 1, w).astype(jnp.float32)[None, :, None]
        outs.append(tot / cnt)
    pooled = jnp.concatenate(outs, axis=-1) - u.astype(jnp.float32)
    return pooled.astype(u.dtype), ext[:, -POOL_HIST:].astype(u.dtype)

def merge_and_ffn(x, a_out, pooled, ga, gb, w_attn_up, w_pool, pool_scale, w_out,
                  g_mix_post, g_ffn_pre, w_ff1, w_ff2, g_ffn_post):
    B, T, _ = x.shape
    br_a = a_out @ w_attn_up
    br_b = jnp.einsum('btgc,gcd->btgd', pooled.reshape(B, T, POOL_GROUPS, POOL_GW),
                      w_pool).reshape(B, T, D_MODEL) * pool_scale
    m = jax.nn.sigmoid(ga) * br_a + jax.nn.sigmoid(gb) * br_b
    x = x + rmsnorm(m @ w_out, g_mix_post)
    h = rmsnorm(x, g_ffn_pre)
    z = jnp.square(jax.nn.relu(h @ w_ff1))
    return x + rmsnorm(z @ w_ff2, g_ffn_post)

def setup_inputs(seed: int = 0) -> dict:
    key = jax.random.key(seed)
    ks = jax.random.split(key, 24)
    f32 = jnp.float32
    nrm = lambda k, s, sc: jax.random.normal(k, s, f32) * sc
    gain = lambda k: 1.0 + 0.1 * jax.random.normal(k, (DEPTH, D_MODEL), f32)
    return {
        "x_prompt": nrm(ks[0], (BATCH, SEQ, D_MODEL), 1.0),
        "x_sample": nrm(ks[1], (DEC_BATCH, DEC_SEQ, D_MODEL), 1.0),
        "cache_k": nrm(ks[2], (DEPTH, DEC_BATCH, PAST_LEN, N_HEADS, HEAD_DIM), 1.0),
        "cache_v": nrm(ks[3], (DEPTH, DEC_BATCH, PAST_LEN, N_HEADS, HEAD_DIM), 1.0),
        "cache_logf": jax.nn.log_sigmoid(3.0 + nrm(ks[4], (DEPTH, DEC_BATCH, PAST_LEN, N_HEADS), 1.0)),
        "state_pool": nrm(ks[5], (DEPTH, DEC_BATCH, POOL_HIST, POOL_W), 1.0),
        "g_mix_pre": gain(ks[6]),
        "w_in": nrm(ks[7], (DEPTH, D_MODEL, IN_W), D_MODEL ** -0.5),
        "b_f": 3.0 + nrm(ks[8], (DEPTH, N_HEADS), 0.1),
        "w_attn_up": nrm(ks[9], (DEPTH, ATTN_W, D_MODEL), ATTN_W ** -0.5),
        "w_pool": nrm(ks[10], (DEPTH, POOL_GROUPS, POOL_GW, POOL_OUT_GW), POOL_GW ** -0.5),
        "pool_scale": gain(ks[11]),
        "w_out": nrm(ks[12], (DEPTH, D_MODEL, D_MODEL), D_MODEL ** -0.5),
        "g_mix_post": gain(ks[13]),
        "g_ffn_pre": gain(ks[14]),
        "w_ff1": nrm(ks[15], (DEPTH, D_MODEL, D_FF), D_MODEL ** -0.5),
        "w_ff2": nrm(ks[16], (DEPTH, D_FF, D_MODEL), D_FF ** -0.5),
        "g_ffn_post": gain(ks[17]),
    }

def reference(x_prompt, x_sample, cache_k, cache_v, cache_logf, state_pool,
              g_mix_pre, w_in, b_f, w_attn_up, w_pool, pool_scale, w_out,
              g_mix_post, g_ffn_pre, w_ff1, w_ff2, g_ffn_post):
    xp, xs = x_prompt, x_sample
    Bp, Tp, _ = xp.shape
    Bs, Ts, _ = xs.shape
    kp_l, vp_l, fp_l, pp_l, ks_l, vs_l, fs_l, ps_l = [], [], [], [], [], [], [], []
    for l in range(DEPTH):
        h = rmsnorm(xp, g_mix_pre[l])
        q, k, v, logf, u, ga, gb = split_projection(h, w_in[l], b_f[l])
        a_out = fox_prompt(q, k, v, logf)
        pooled, pool_new = multi_scale_pool(jnp.zeros((Bp, POOL_HIST, POOL_W), u.dtype), u,
                                            jnp.arange(Tp))
        xp = merge_and_ffn(xp, a_out, pooled, ga, gb, w_attn_up[l], w_pool[l], pool_scale[l],
                           w_out[l], g_mix_post[l], g_ffn_pre[l], w_ff1[l], w_ff2[l], g_ffn_post[l])
        kp_l.append(k); vp_l.append(v); fp_l.append(logf); pp_l.append(pool_new)

        past = cache_k.shape[2]
        h = rmsnorm(xs, g_mix_pre[l])
        q, k, v, logf, u, ga, gb = split_projection(h, w_in[l], b_f[l])
        k_all = jnp.concatenate([cache_k[l].astype(k.dtype), k], axis=1)
        v_all = jnp.concatenate([cache_v[l].astype(v.dtype), v], axis=1)
        f_all = jnp.concatenate([cache_logf[l].astype(jnp.float32), logf], axis=1)
        a_out = fox_sample(q, k_all, v_all, f_all, past)
        pooled, pool_new = multi_scale_pool(state_pool[l], u, past + jnp.arange(Ts))
        xs = merge_and_ffn(xs, a_out, pooled, ga, gb, w_attn_up[l], w_pool[l], pool_scale[l],
                           w_out[l], g_mix_post[l], g_ffn_pre[l], w_ff1[l], w_ff2[l], g_ffn_post[l])
        ks_l.append(k); vs_l.append(v); fs_l.append(logf); ps_l.append(pool_new)

    k_prompt = jnp.stack(kp_l, 0)
    v_prompt = jnp.stack(vp_l, 0)
    logf_prompt = jnp.stack(fp_l, 0)
    pool_prompt = jnp.stack(pp_l, 0)
    k_sample = jnp.stack(ks_l, 0)
    v_sample = jnp.stack(vs_l, 0)
    logf_sample = jnp.stack(fs_l, 0)
    pool_sample = jnp.stack(ps_l, 0)
    return (xp, xs, k_prompt, v_prompt, logf_prompt, pool_prompt,
            k_sample, v_sample, logf_sample, pool_sample)


_drawn_inputs = setup_inputs


def setup_inputs(seed=0):
    import zlib

    import numpy as np

    out = dict(_drawn_inputs(seed))
    spreads = {}
    factors = {}
    for name, (base, spread) in spreads.items():
        noise = np.random.default_rng([zlib.crc32(name.encode()), seed]).standard_normal(out[name].shape)
        drawn = base * np.exp(spread * noise) if base else spread * noise
        out[name] = __import__('jax').numpy.asarray(drawn.astype(out[name].dtype))
    for name, factor in factors.items():
        out[name] = (out[name] * factor).astype(out[name].dtype)
    return out
```

```python
from contextlib import ExitStack

import concourse.bass as bass
from concourse import mybir

F32 = mybir.dt.float32
F32R = mybir.dt.float32r
I32 = mybir.dt.int32
ALU = mybir.AluOpType
ACT = mybir.ActivationFunctionType

P = 128
D = 2048
KD = D // P
SEQ = 256
BD = 8
QS = 16
PAST = 256
T = SEQ + BD * QS
TT = T // P
H = 16
HD = 64
PAIRS = H // 2
AW = H * HD
POOLW = 1024
PC = POOLW // P
HIST = 15
GROUPS = 4
DFF = 4 * D
EPS = 1e-6
SCALE = HD ** -0.5
OFF_K, OFF_V, OFF_F = AW, 2 * AW, 3 * AW
OFF_U = OFF_F + H
OFF_GA = OFF_U + POOLW
OFF_GB = OFF_GA + D
MASKED = -1e30
LOWEST = -3e38

UW = 1024
RING = 4
AHEAD = 2
CHUNK = 1024
NCHUNK = DFF // CHUNK
BATCH_KEYS = PAST // P
SCOL = PAST + P

U_F = 0
U_U = U_F + 2
U_POOL = U_U + 4 * GROUPS
U_HP = U_POOL + GROUPS
U_GATE = U_HP + 6 * PAIRS
U_OUT = U_GATE + 10 * (KD // 2)
U_FFN = U_OUT + 8 * 4
UNITS = U_FFN + 32 * NCHUNK


def streaming_encoder(nc, x_prompt, x_sample, cache_k, cache_v, cache_logf, state_pool,
                      g_mix_pre, w_in, b_f, w_attn_up, w_pool, pool_scale, w_out,
                      g_mix_post, g_ffn_pre, w_ff1, w_ff2, g_ffn_post,
                      y_prompt, y_sample, k_prompt, v_prompt, logf_prompt, pool_prompt,
                      k_sample, v_sample, logf_sample, pool_sample):
    xp_v = x_prompt.rearrange("o (t p) d -> p (o t) d", p=P)
    xs_v = x_sample.rearrange("b q d -> (b q) d")
    win_v = w_in.rearrange("o (k p) n -> p (o k) n", p=P)
    wup_v = w_attn_up.rearrange("o (k p) n -> p (o k) n", p=P)
    wpool_v = w_pool.rearrange("o g (k p) n -> g p (o k) n", p=P)
    wout_v = w_out.rearrange("o (k p) n -> p (o k) n", p=P)
    wff1_v = w_ff1.rearrange("o (k p) n -> p (o k) n", p=P)
    wff2_v = w_ff2.rearrange("o (k p) n -> p (o k) n", p=P)
    ck_v = cache_k.rearrange("o b (t p) h d -> p (o b t) (h d)", p=P)
    cv_v = cache_v.rearrange("o b (t p) h d -> p (o b t) (h d)", p=P)
    clf_v = cache_logf.rearrange("o b (t p) h -> t p (o b) h", p=P)
    kp_v = k_prompt.rearrange("l o (t p) h d -> p (l o t) (h d)", p=P)
    vp_v = v_prompt.rearrange("l o (t p) h d -> p (l o t) (h d)", p=P)
    ks_v = k_sample.rearrange("l b q h d -> (l b q) (h d)")
    vs_v = v_sample.rearrange("l b q h d -> (l b q) (h d)")
    yp_v = y_prompt.rearrange("o (t p) d -> p (o t) d", p=P)
    ys_v = y_sample.rearrange("b q d -> (b q) d")
    lfp_v = logf_prompt.rearrange("l o (t p) h -> p (l o t) h", p=P)
    lfs_v = logf_sample.rearrange("l b q h -> (l b q) h")
    ncp_dram = nc.dram_tensor("ncp_dram", [H, SEQ], F32, kind="Internal").ap()
    ncs_dram = nc.dram_tensor("ncs_dram", [PAIRS, BD, 2, SCOL], F32, kind="Internal").ap()

    BASE = (nc.sbuf_base + 63) // 64 * 64
    at = [0]

    def place(name, shape, dt, offset=None):
        size = 4
        for n in shape[1:]:
            size *= n
        if offset is None:
            offset = at[0]
        at[0] = (offset + size + 31) // 32 * 32
        return nc.alloc_sbuf_tensor_at(name, shape, dt, offset=BASE + offset)

    KB = 1024
    w_raw = place("w_raw", [P, RING, UW], F32)
    w_hi = place("w_hi", [P, RING, UW], F32R)
    w_lo = place("w_lo", [P, RING, UW], F32R)
    ht_hi = place("ht_hi", [P, KD, T], F32R)
    ht_lo = place("ht_lo", [P, KD, T], F32R)
    BRB = at[0]
    brb = place("brb", [P, KD, T], F32)
    xres = place("xres", [P, TT, D], F32, BRB)
    junk0 = place("junk0", [P, D], F32, BRB)
    u_new = place("u_new", [P, PC, BD * QS], F32, BRB + 20 * 1024)
    at[0] = BRB + 24 * 1024
    ATT = at[0]
    at_hi = place("at_hi", [P, PAIRS, T], F32R)
    at_lo = place("at_lo", [P, PAIRS, T], F32R)
    END_ATT = at[0]
    ybuf = place("ybuf", [P, TT, D], F32, ATT)
    f_x = place("f_x", [H, T], F32, ATT)
    f_neg = place("f_neg", [H, T], F32)
    f_abs = place("f_abs", [H, T], F32)
    f_exp = place("f_exp", [H, T], F32)
    f_one = place("f_one", [H, T], F32)
    f_log = place("f_log", [H, T], F32)
    logf_t = place("logf_t", [H, T], F32)
    logf_nat = place("logf_nat", [P, TT, H], F32)
    ncp = place("ncp", [H, SEQ], F32)
    clf = place("clf", [P, BATCH_KEYS, BD * H], F32)
    logf_all = place("logf_all", [P, PAST + QS], F32)
    ncs = place("ncs", [P, SCOL], F32)
    gain_nat = place("gain_nat", [KD, 2, P], F32)
    ones = place("ones", [P, PAST + QS], F32)
    u_nat = place("u_nat", [P, POOLW], F32)
    assert at[0] <= END_ATT
    ident = place("ident", [P, P], F32, END_ATT)
    gains_t = place("gains_t", [P, 2, KD], F32)
    g_pre_t, pscale_t = gains_t[:, 0, :], gains_t[:, 1, :]
    mask_new = place("mask_new", [P, 2, P], F32)
    recip_cnt = place("recip_cnt", [P, GROUPS, 2, HIST], F32)
    first = place("first", [P, GROUPS, 2, HIST], F32)
    bf_t = place("bf_t", [H, 1], F32)
    ssq = place("ssq", [P, 4, TT, 4], F32)
    var = place("var", [P, 4, TT], F32)
    std = place("std", [P, 4, TT], F32)
    rstd = place("rstd", [P, 4, TT], F32)
    row_i = place("row_i", [P, 3], I32)
    row_f = place("row_f", [P, 2], F32)
    col_f = place("col_f", [P, P], F32)
    cnt_f = place("cnt_f", [P, HIST], F32)
    mask_t = place("mask_t", [P, 2, P], F32)
    mx = place("mx", [P, 6], F32)
    nmx = place("nmx", [P, 6], F32)
    esum = place("esum", [P, 6], F32)
    erec = place("erec", [P, 6], F32)
    R = (at[0] + 63) // 64 * 64
    LIMIT = nc.sbuf_usable_end - BASE
    x_sb = place("x_sb", [P, TT, D], F32, R)
    pl_hi = place("pl_hi", [P, PC, T], F32R, R)
    pl_lo = place("pl_lo", [P, PC, T], F32R)
    u_p = place("u_p", [P, PC, HIST + SEQ], F32)
    u_s = place("u_s", [P, PC, BD, HIST + QS], F32)
    win_p = place("win_p", [P, 2, 2, HIST + SEQ], F32)
    win_s = place("win_s", [P, 2, 2, BD, HIST + QS], F32)
    st_nat = place("st_nat", [BD * HIST, POOLW], F32)
    pooled = place("pooled", [P, 2, T], F32, at[0] - 4 * KB)
    un_p = place("un_p", [QS, POOLW], F32, at[0])
    
    kc = place("kc", [P, BD * BATCH_KEYS, P], F32, R)
    vc = place("vc", [P, BD * BATCH_KEYS, P], F32)
    kts = place("kts", [P, 4, PAST], F32)
    qp = [place(f"qp{n}", [P, 2, SEQ], F32) for n in range(2)]
    qs = [place(f"qs{n}", [P, BD, 2, QS], F32) for n in range(2)]
    kt = [place(f"kt{n}", [P, T], F32) for n in range(2)]
    vt = place("vt", [P, T], F32)
    k_nat = place("k_nat", [P, TT, P], F32)
    v_nat = place("v_nat", [P, TT, P], F32)
    bias_p = place("bias_p", [P, 2, SEQ], F32)
    bias_0 = place("bias_0", [P, 2, P], F32)
    bias_s = place("bias_s", [P, 2, SCOL], F32)
    s_p = place("s_p", [P, 2, P + SEQ], F32)
    s_s = place("s_s", [P, 2, SCOL], F32)
    pt_p = place("pt_p", [P, 2, P + SEQ], F32)
    pt_s = place("pt_s", [P, 2, SCOL], F32)
    o_nat = place("o_nat", [P, 2, P], F32)
    assert at[0] <= LIMIT, (at[0], LIMIT)
    sg_a = place("sg_a", [P, 2, T], F32, R)
    sg_b = place("sg_b", [P, 2, T], F32)
    mt_hi = place("mt_hi", [P, KD, T], F32R, R + 8 * KB)
    mt_lo = place("mt_lo", [P, KD, T], F32R)
    junk = place("junk", [P, 512], F32)
    assert at[0] <= LIMIT
    g_post_r = place("g_post_r", [P, D], F32, R)
    g_fpre_r = place("g_fpre_r", [P, D], F32, R + 8 * KB)
    g_fpost_r = place("g_fpost_r", [P, D], F32, R + 16 * KB)
    z_hi = place("z_hi", [P, CHUNK // P, T], F32R)
    z_lo = place("z_lo", [P, CHUNK // P, T], F32R)
    z_relu = place("z_relu", [P, 2, T], F32)
    z_sq = place("z_sq", [P, 2, T], F32)
    junk2 = place("junk2", [P, D], F32, R + 24 * KB)

    with ExitStack() as ctx:
        ps = ctx.enter_context(nc.psum_tensor("ps", [P, 8, 512], F32))

        def sem(name):
            return ctx.enter_context(nc.semaphore(name))

        def sems(name, n):
            return [sem(f"{name}{i}") for i in range(n)]

        G = [0, 1]
        TP = [2, 3]
        S = [4, 5, 6, 7]

        raw_landed = sems("raw_landed", RING)
        hi_ready = sem("hi_ready")
        lo_ready = sem("lo_ready")
        unit_used = sem("unit_used")
        x_landed = sems("x_landed", TT)
        small_landed = sem("small_landed")
        state_landed = sem("state_landed")
        clf_landed = sem("clf_landed")
        pool_const = sem("pool_const")
        dve_const = sem("dve_const")
        sp_waited, dve_waited, pool_waited = sem("sp_waited"), sem("dve_waited"), sem("pool_waited")
        ssq_ready = sems("ssq_ready", 4)
        var_ready = sems("var_ready", 4)
        std_ready = sems("std_ready", 4)
        rstd_ready = sems("rstd_ready", 4)
        xn_ready = sem("xn_ready")
        gain_psum, gain_ready = sem("gain_psum"), sem("gain_ready")
        ht_psum = sem("ht_psum")
        ht_hi_ready = sem("ht_hi_ready")
        ht_lo_ready = sem("ht_lo_ready")
        aux_psum = sem("aux_psum")
        aux_saved = sem("aux_saved")
        f_dve = sem("f_dve")
        f_act = sem("f_act")
        fnat_psum = sem("fnat_psum")
        fnat_saved = sem("fnat_saved")
        logf_new_in = sem("logf_new_in")
        ncp_ready = sem("ncp_ready")
        ncs_ready = sem("ncs_ready")
        nc_stored = sem("nc_stored")
        u_saved = sem("u_saved")
        win_level = sem("win_level")
        ident_zero = sem("ident_zero")
        win_step = sem("win_step")
        pooled_ready = sem("pooled_ready")
        pl_hi_ready = sem("pl_hi_ready")
        pl_lo_ready = sem("pl_lo_ready")
        brb_psum = sem("brb_psum")
        brb_act = sem("brb_act")
        brb_dve = sem("brb_dve")
        unat_psum = sem("unat_psum")
        unat_saved = sem("unat_saved")
        q_saved, k_saved, v_saved = sem("q_saved"), sem("k_saved"), sem("v_saved")
        q_zero = sem("q_zero")
        tp_full = sems("tp_full", 2)
        tp_free = sems("tp_free", 2)
        s_full = sems("s_full", 4)
        kc_landed, vc_landed = sem("kc_landed"), sem("vc_landed")
        bias_landed = sem("bias_landed")
        bias_ready = sem("bias_ready")
        max_ready = sem("max_ready")
        nmx_ready = sem("nmx_ready")
        exp_ready = sem("exp_ready")
        erec_ready = sem("erec_ready")
        prob_ready = sem("prob_ready")
        srec_ready = sem("srec_ready")
        onat_ready = sem("onat_ready")
        k_stored, v_stored = sem("k_stored"), sem("v_stored")
        a_hi_ready, a_lo_ready = sem("a_hi_ready"), sem("a_lo_ready")
        ga_ready, gb_ready = sem("ga_ready"), sem("gb_ready")
        ta_ready, tb_ready = sem("ta_ready"), sem("tb_ready")
        m_ready = sem("m_ready")
        m_hi_ready, m_lo_ready = sem("m_hi_ready"), sem("m_lo_ready")
        y_saved = sem("y_saved")
        xres_landed = sem("xres_landed")
        gpost_landed = sem("gpost_landed")
        gfpre_landed = sem("gfpre_landed")
        gfpost_landed = sem("gfpost_landed")
        yn_ready, x2_ready, hn_ready = sem("yn_ready"), sem("x2_ready"), sem("hn_ready")
        h2_psum = sem("h2_psum")
        h2_hi_ready, h2_lo_ready = sem("h2_hi_ready"), sem("h2_lo_ready")
        acc_zero = sem("acc_zero")
        relu_ready = sem("relu_ready")
        sq_ready = sem("sq_ready")
        z_hi_ready, z_lo_ready = sem("z_hi_ready"), sem("z_lo_ready")
        o_added = sem("o_added")
        on_ready, out_ready = sem("on_ready"), sem("out_ready")
        pool_stored, logf_stored = sem("pool_stored"), sem("logf_stored")
        stored = sem("stored")

        block = ctx.enter_context(nc.Block())

        def f32(ap):
            return ap.bitcast(F32)

        def later(index):
            return not isinstance(index, int) or index > 0

        @block.sync
        def _(sp):
            def load(n, more, src, k, w, apart=False):
                slot = n % RING
                if n >= RING:
                    sp.wait_ge(lo_ready, n - RING + 1 + more)
                    if apart:
                        sp.sem_inc(sp_waited, 1)
                dst = w_raw[:, slot, :].rearrange("p (k w) -> p k w", w=w)
                sp.dma_start(dst, src).then_inc(raw_landed[slot], 16)

            def win(k0, nk, c0, w):
                return win_v[:, k0:k0 + nk, bass.ds(c0, w)]

            for n in range(2):
                load(U_F + n, 0, win(8 * n, 8, OFF_F, P), 8, P)
            for g in range(GROUPS):
                for n in range(4):
                    load(U_U + 4 * g + n, 0, win(4 * n, 4, OFF_U + 256 * g, 256), 4, 256)
            for g in range(GROUPS):
                load(U_POOL + g, 0, wpool_v[g], 2, 512)

            def head_pair(n, more, hp):
                for part in range(3):
                    for half in range(2):
                        load(n + 2 * part + half, more, win(8 * half, 8, hp * P + part * AW, P), 8, P)

            for hp in range(2):
                head_pair(U_HP + 6 * hp, 0, hp)
            with sp.Fori(0, 3) as i:
                for j in range(2):
                    head_pair(U_HP + 12 + 6 * j, i * 12, i * 2 + (2 + j))

            def gate_pair(n, more, jp):
                for q in range(4):
                    load(n + q, more, win(4 * q, 4, jp * 256 + OFF_GA, 256), 4, 256)
                for q in range(4):
                    load(n + 4 + q, more, win(4 * q, 4, jp * 256 + OFF_GB, 256), 4, 256)
                for q in range(2):
                    load(n + 8 + q, more, wup_v[:, 4 * q:4 * q + 4, bass.ds(jp * 256, 256)], 4, 256,
                         apart=q == 0)

            for jp in range(2):
                gate_pair(U_GATE + 10 * jp, 0, jp)
            with sp.Fori(0, 3) as i:
                for j in range(2):
                    gate_pair(U_GATE + 20 + 10 * j, i * 20, i * 2 + (2 + j))
            with sp.Fori(0, 2) as i:
                for j in range(2):
                    for q in range(8):
                        load(U_OUT + 8 * j + q, i * 16,
                             wout_v[:, 2 * q:2 * q + 2, bass.ds(i * 1024 + 512 * j, 512)], 2, 512)
            with sp.Fori(0, NCHUNK) as c:
                for pr in range(4):
                    for q in range(4):
                        load(U_FFN + 4 * pr + q, c * 32,
                             wff1_v[:, 4 * q:4 * q + 4, bass.ds(c * CHUNK + 256 * pr, 256)], 4, 256)
                for cg in range(4):
                    for q in range(4):
                        load(U_FFN + 16 + 4 * cg + q, c * 32,
                             wff2_v[:, bass.ds(c * 8 + 2 * q, 2), 512 * cg:512 * cg + 512], 2, 512)

            for t in range(TT):
                sp.wait_ge(out_ready, t + 1)
                sp.dma_start(yp_v[:, t, :] if t < 2 else ys_v, ybuf[:, t, :]).then_inc(stored, 16)
            sp.wait_ge(stored, 16 * TT)

        @block.tensor
        def _(pe):
            def unit(n, more):
                pe.wait_ge(lo_ready, n + 1 + more)
                return n % RING

            def across(n, more, bank, tiles, k0, nk, x_hi, x_lo, k_last, parts=(0, 1)):
                slot = unit(n, more)
                w = tiles * P
                wh = w_hi[:, slot, :].rearrange("p (k w) -> p k w", w=w)
                wl = w_lo[:, slot, :].rearrange("p (k w) -> p k w", w=w)
                last = None
                for k in range(nk // 2 * parts[0], nk // 2 * (parts[-1] + 1)):
                    for c in range(tiles):
                        out = ps[:, bank + c, 0:T]
                        cols = slice(c * P, (c + 1) * P)
                        kk = k0 + k
                        pe.matmul(out, wh[:, k, cols], x_hi[:, kk, :], start=(kk == 0), stop=False)
                        pe.matmul(out, wh[:, k, cols], x_lo[:, kk, :], start=False, stop=False)
                        last = pe.matmul(out, wl[:, k, cols], x_hi[:, kk, :], start=False,
                                         stop=(kk == k_last))
                if parts[-1] == 1:
                    last.then_inc(unit_used, 1)
                return last

            def down(n, more, banks, k0, x_hi, x_lo, k_last):
                slot = unit(n, more)
                wh = w_hi[:, slot, :].rearrange("p (k w) -> p k w", w=512)
                wl = w_lo[:, slot, :].rearrange("p (k w) -> p k w", w=512)
                for k in range(2):
                    kk = k0 + k
                    for t in range(TT):
                        out = ps[:, banks[t], :]
                        rows = slice(t * P, (t + 1) * P)
                        pe.matmul(out, x_hi[:, kk, rows], wh[:, k, :], start=(kk == 0), stop=False)
                        pe.matmul(out, x_hi[:, kk, rows], wl[:, k, :], start=False, stop=False)
                        last = pe.matmul(out, x_lo[:, kk, rows], wh[:, k, :], start=False,
                                         stop=(kk == k_last))
                last.then_inc(unit_used, 1)
                return last

            pe.wait_ge(pool_const, 1)
            pe.wait_ge(small_landed, 48)
            for n in range(2):
                last = pe.transpose(ps[:, 0, n * KD:(n + 1) * KD], gain_nat[:, n, :], ident[0:KD, 0:KD])
            last.then_inc(gain_psum, 1)
            pe.wait_ge(xn_ready, TT)
            for k in range(KD):
                if k >= 6:
                    pe.wait_ge(ht_lo_ready, k - 5)
                for t in range(TT):
                    last = pe.transpose(ps[:, 2 + k % 6, t * P:(t + 1) * P],
                                        x_sb[:, t, k * P:(k + 1) * P], ident[:, :])
                last.then_inc(ht_psum, 1)
            pe.wait_ge(state_landed, 16)
            for n in range(2):
                pe.wait_ge(ht_lo_ready, KD + n - 5)
                for c in range(4):
                    last = pe.transpose(ps[:, 6 + n, c * P:c * P + BD * HIST],
                                        st_nat[:, (4 * n + c) * P:(4 * n + c + 1) * P],
                                        ident[0:BD * HIST, 0:BD * HIST])
                last.then_inc(aux_psum, 1)
            pe.wait_ge(clf_landed, 32)
            pe.wait_ge(ht_lo_ready, KD + 2 - 5)
            for t in range(BATCH_KEYS):
                last = pe.transpose(ps[:, 2, t * P:(t + 1) * P], clf[:, t, :], ident[:, :])
            last.then_inc(aux_psum, 1)

            pe.wait_ge(ht_lo_ready, KD)
            across(U_F, 0, 0, 1, 0, 8, ht_hi, ht_lo, KD - 1)
            across(U_F + 1, 0, 0, 1, 8, 8, ht_hi, ht_lo, KD - 1)

            for g in range(GROUPS):
                if g == 0:
                    pass
                elif g == 1:
                    pe.wait_ge(aux_saved, 2)
                else:
                    pe.wait_ge(u_saved, 2 * (g - 1))
                for q in range(4):
                    across(U_U + 4 * g + q, 0, 4 + 2 * (g % 2), 2, 4 * q, 4, ht_hi, ht_lo, KD - 1)
                if g == 1:
                    pe.wait_ge(f_dve, 12)
                    for t in range(TT):
                        last = pe.transpose(ps[:, 3, t * H:(t + 1) * H], logf_t[:, t * P:(t + 1) * P],
                                            ident[0:H, 0:H])
                    last.then_inc(fnat_psum, 1)

            for g in range(GROUPS):
                pe.wait_ge(pl_lo_ready, g + 1)
                slot = unit(U_POOL + g, 0)
                wh = w_hi[:, slot, :].rearrange("p (k w) -> p k w", w=512)
                wl = w_lo[:, slot, :].rearrange("p (k w) -> p k w", w=512)
                for j in range(4):
                    if g == 0:
                        pe.wait_ge([f_dve, f_dve, aux_saved, fnat_saved][j], [1, 1, 3, 1][j])
                    else:
                        pe.wait_ge([brb_act, brb_act, brb_dve, brb_dve][j], 2 * (g - 1) + 1 + j % 2)
                    for k in range(2):
                        cols = slice(j * P, (j + 1) * P)
                        kk = 2 * g + k
                        pe.matmul(ps[:, j, 0:T], wh[:, k, cols], pl_hi[:, kk, :], start=(k == 0), stop=False)
                        pe.matmul(ps[:, j, 0:T], wh[:, k, cols], pl_lo[:, kk, :], start=False, stop=False)
                        last = pe.matmul(ps[:, j, 0:T], wl[:, k, cols], pl_hi[:, kk, :], start=False,
                                         stop=(k == 1))
                    if j < 3:
                        last.then_inc(brb_psum, 1)
                last.then_inc(unit_used, 1)
                if g == 0:
                    pe.wait_ge(u_saved, 2 * GROUPS)
                    for n in range(2):
                        for c in range(4):
                            last = pe.transpose(ps[0:QS, 4 + n, c * P:(c + 1) * P],
                                                u_p[:, 4 * n + c, HIST + SEQ - QS:HIST + SEQ], ident[:, :])
                        last.then_inc(unat_psum, 1)
                    for n in range(2):
                        for c in range(4):
                            last = pe.transpose(ps[:, 6 + n, c * P:(c + 1) * P], u_new[:, 4 * n + c, :],
                                                ident[:, :])
                        last.then_inc(unat_psum, 1)

            def rows_back(a, par):
                pe.wait_ge(k_saved, a + 1)
                pe.wait_ge(v_saved, a + 1)
                for x, src in ((0, kt[par]), (1, vt)):
                    if later(a):
                        pe.wait_ge(tp_free[x], a * 5)
                    for t in range(TT):
                        last = pe.transpose(ps[:, TP[x], t * P:(t + 1) * P], src[:, t * P:(t + 1) * P],
                                            ident[:, :])
                    last.then_inc(tp_full[x], 1)

            def scores_prompt(a, par):
                pe.wait_ge(q_saved, a + 1)
                if later(a):
                    pe.wait_ge(a_lo_ready, a * 2)
                for h in range(2):
                    last = pe.matmul(ps[:, S[0], h * P:(h + 1) * P], qp[par][:, h, 0:P], kt[par][:, 0:P],
                                     start=True, stop=True)
                last.then_inc(s_full[0], 1)
                if later(a):
                    pe.wait_ge(onat_ready, a)
                for h in range(2):
                    last = pe.matmul(ps[:, S[1], h * SEQ:(h + 1) * SEQ], qp[par][:, h, P:SEQ],
                                     kt[par][:, 0:SEQ], start=True, stop=True)
                last.then_inc(s_full[1], 1)

            def cache_keys(a, half):
                if half == 0:
                    pe.wait_ge(kc_landed, a * 16 + 16)
                for x in range(2):
                    pe.wait_ge(tp_free[x], a * 5 + 1 + half)
                    for n in range(4):
                        tile = (4 * half + 2 * x) * BATCH_KEYS + n
                        last = pe.transpose(ps[:, TP[x], n * P:(n + 1) * P], kc[:, tile, :], ident[:, :])
                    last.then_inc(tp_full[x], 1)

            def scores_sample(a, par, half):
                bank = S[2 + half]
                if half == 0:
                    if later(a):
                        pe.wait_ge(a_lo_ready, a * 2)
                else:
                    if later(a):
                        pe.wait_ge(max_ready, a * 6)
                pe.wait_ge(tp_free[0], a * 5 + 2 + half)
                pe.wait_ge(tp_free[1], a * 5 + 2 + half)
                pe.matmul(ps[:, bank, PAST:SCOL],
                          qs[par][:, 4 * half:4 * half + 4, :, :].rearrange("p b h q -> p (b h q)"),
                          kt[par][:, SEQ:T], start=True, stop=True)
                for b in range(4):
                    last = pe.matmul(ps[32 * b:32 * b + 32, bank, 0:PAST],
                                     qs[par][:, 4 * half + b, :, :].rearrange("p h q -> p (h q)"),
                                     kts[:, b, :], start=True, stop=True, tile_position=(0, 32 * b))
                last.then_inc(s_full[2 + half], 1)

            def turn_prompt(a):
                pe.wait_ge(prob_ready, a + 1)
                for x in range(2):
                    pe.wait_ge(tp_free[x], a * 5 + 3)
                    for n in range(3):
                        last = pe.transpose(ps[:, TP[x], n * P:(n + 1) * P], s_p[:, x, n * P:(n + 1) * P],
                                            ident[:, :])
                    last.then_inc(tp_full[x], 1)

            def turn_sample(a):
                for x in range(2):
                    pe.wait_ge(exp_ready, a * 6 + 5 + x)
                    pe.wait_ge(tp_free[x], a * 5 + 4)
                    for n in range(3):
                        last = pe.transpose(ps[:, TP[x], n * P:(n + 1) * P], s_s[:, x, n * P:(n + 1) * P],
                                            ident[:, :])
                    last.then_inc(tp_full[x], 1)

            def mix_prompt(a):
                pe.wait_ge(tp_free[0], a * 5 + 4)
                pe.wait_ge(tp_free[1], a * 5 + 4)
                pe.wait_ge(max_ready, a * 6 + 2)
                for h in range(2):
                    rows = slice(HD * h, HD * (h + 1))
                    pe.matmul(ps[rows, S[0], 0:P], v_nat[:, 0, rows], pt_p[:, h, 0:P],
                              start=True, stop=True, tile_position=(0, HD * h))
                    pe.matmul(ps[rows, S[0], P:SEQ], v_nat[:, 0, rows], pt_p[:, h, P:SEQ],
                              start=True, stop=False, tile_position=(0, HD * h))
                    last = pe.matmul(ps[rows, S[0], P:SEQ], v_nat[:, 1, rows], pt_p[:, h, SEQ:SEQ + P],
                                     start=False, stop=True, tile_position=(0, HD * h))
                last.then_inc(s_full[0], 1)

            def mix_sample(a):
                pe.wait_ge(tp_free[0], a * 5 + 5)
                pe.wait_ge(tp_free[1], a * 5 + 5)
                pe.wait_ge(vc_landed, a * 16 + 16)
                pe.wait_ge(max_ready, a * 6 + 4)
                for half in range(2):
                    cols = slice(half * P, (half + 1) * P)
                    for b in range(4):
                        for t in range(BATCH_KEYS):
                            rows = slice(32 * b, 32 * b + 32)
                            pe.matmul(ps[rows, S[1], cols],
                                      pt_s[:, half, t * P + 32 * b:t * P + 32 * b + 32],
                                      vc[:, (4 * half + b) * BATCH_KEYS + t, :],
                                      start=(t == 0), stop=(t == BATCH_KEYS - 1), tile_position=(0, 32 * b))
                    last = pe.matmul(ps[:, S[1], cols], pt_s[:, half, PAST:SCOL], v_nat[:, 2, :],
                                     start=False, stop=True, skip_group_check=True)
                last.then_inc(s_full[1], 1)

            def turn_out(a):
                pe.wait_ge(onat_ready, a + 1)
                pe.wait_ge(max_ready, a * 6 + 5)
                for half in range(2):
                    last = pe.transpose(ps[:, S[2], half * P:(half + 1) * P], o_nat[:, half, :], ident[:, :])
                last.then_inc(s_full[2], 1)

            def proj(n, more, hp, half, which, parts=(0, 1)):
                if half == 0 and parts[0] == 0:
                    if which == 0 and later(hp):
                        pe.wait_ge(k_saved, hp)
                    if which == 1 and later(hp):
                        pe.wait_ge(v_saved, hp)
                    if which == 2:
                        pe.wait_ge(q_saved, hp + 1)
                bank = G[(par_of[0] + which) % 2]
                across(n, more, bank, 1, 8 * half, 8, ht_hi, ht_lo, KD - 1, parts)

            par_of = [0]

            def head_pair(n, more, hp, par, attend):
                par_of[0] = par
                a, pa = hp - 1, 1 - par
                proj(n, more, hp, 0, 0)
                if attend:
                    rows_back(a, pa)
                    scores_prompt(a, pa)
                proj(n + 1, more, hp, 1, 0)
                if attend:
                    cache_keys(a, 0)
                proj(n + 2, more, hp, 0, 1)
                if attend:
                    scores_sample(a, pa, 0)
                    cache_keys(a, 1)
                proj(n + 3, more, hp, 1, 1)
                if attend:
                    scores_sample(a, pa, 1)
                    turn_prompt(a)
                proj(n + 4, more, hp, 0, 2)
                if attend:
                    turn_sample(a)
                    mix_prompt(a)
                proj(n + 5, more, hp, 1, 2, (0,))
                if attend:
                    mix_sample(a)
                proj(n + 5, more, hp, 1, 2, (1,))
                if attend:
                    turn_out(a)

            pe.wait_ge(brb_act, 2 * GROUPS)
            pe.wait_ge(brb_dve, 2 * GROUPS)
            pe.wait_ge(unat_saved, 4)
            head_pair(U_HP, 0, 0, 0, False)
            head_pair(U_HP + 6, 0, 1, 1, True)
            with pe.Fori(0, 3) as i:
                for j in range(2):
                    head_pair(U_HP + 12 + 6 * j, i * 12, i * 2 + (2 + j), j, True)

            def gate_a(n, more, q):
                return across(n + q, more, 0, 2, 4 * q, 4, ht_hi, ht_lo, KD - 1)

            def gate_b(n, more, jp):
                for q in range(4):
                    across(n + 4 + q, more, 2, 2, 4 * q, 4, ht_hi, ht_lo, KD - 1)

            def branch_a(n, more, jp):
                for q in range(2):
                    across(n + 8 + q, more, 4, 2, 4 * q, 4, at_hi, at_lo, PAIRS - 1)

            def gate_pair(n, more, jp):
                pe.wait_ge(ga_ready, jp)
                for q in range(4):
                    gate_a(n, more, q)
                pe.wait_ge(gb_ready, jp)
                gate_b(n, more, jp)
                pe.wait_ge(ta_ready, jp)
                branch_a(n, more, jp)

            pe.wait_ge(q_saved, 8)
            pe.wait_ge(k_saved, 8)
            pe.wait_ge(v_saved, 8)
            gate_a(U_GATE, 0, 0)
            rows_back(7, 1)
            scores_prompt(7, 1)
            gate_a(U_GATE, 0, 1)
            cache_keys(7, 0)
            gate_a(U_GATE, 0, 2)
            scores_sample(7, 1, 0)
            cache_keys(7, 1)
            gate_a(U_GATE, 0, 3)
            scores_sample(7, 1, 1)
            turn_prompt(7)
            turn_sample(7)
            mix_prompt(7)
            mix_sample(7)
            turn_out(7)
            pe.wait_ge(tp_free[0], 8 * 5)
            pe.wait_ge(tp_free[1], 8 * 5)
            gate_b(U_GATE, 0, 0)
            pe.wait_ge(a_lo_ready, 16)
            branch_a(U_GATE, 0, 0)
            gate_pair(U_GATE + 10, 0, 1)
            with pe.Fori(0, 3) as i:
                for j in range(2):
                    gate_pair(U_GATE + 20 + 10 * j, i * 20, i * 2 + (2 + j))

            pe.wait_ge(m_lo_ready, KD // 2)
            for i in range(2):
                for j in range(2):
                    if later(i):
                        pe.wait_ge(y_saved, i * 6 - 3 + 3 * j)
                    for q in range(8):
                        down(U_OUT + 8 * j + q, i * 16, [3 * j, 3 * j + 1, 3 * j + 2], 2 * q,
                             mt_hi, mt_lo, KD - 1)

            for t in range(TT):
                pe.wait_ge(hn_ready, t + 1)
                for n in range(4):
                    use = 4 * t + n
                    bank = [6, 7, 0, 1, 2, 3][use % 6]
                    if use >= 6:
                        pe.wait_ge(h2_lo_ready, use - 5)
                    elif use >= 2:
                        pe.wait_ge(y_saved, 12)
                    for c in range(4):
                        k = 4 * n + c
                        last = pe.transpose(ps[:, bank, c * P:(c + 1) * P],
                                            ybuf[:, t, k * P:(k + 1) * P], ident[:, :])
                    last.then_inc(h2_psum, 1)

            pe.wait_ge(h2_lo_ready, 4 * TT)
            def chunk(c):
                for pr in range(4):
                    if pr == 1 and later(c):
                        pe.wait_ge(o_added, c * 12)
                    elif pr >= 2:
                        pe.wait_ge(relu_ready, c * 4 + (pr - 1))
                    elif pr == 0 and later(c):
                        pe.wait_ge(relu_ready, c * 4)
                    for q in range(4):
                        across(U_FFN + 4 * pr + q, c * 32, 2 - 2 * (pr % 2), 2, 4 * q, 4,
                               ht_hi, ht_lo, KD - 1)
                for cg in range(4):
                    banks = [[4, 5, 6], [7, 0, 1]][cg % 2]
                    if cg == 0 and later(c):
                        pe.wait_ge(o_added, c * 12)
                    elif cg == 1:
                        pe.wait_ge(relu_ready, c * 4 + 4)
                    elif cg >= 2:
                        pe.wait_ge(o_added, c * 12 + 3 * (cg - 1))
                    for q in range(4):
                        if cg == 0:
                            pe.wait_ge(z_lo_ready, c * 4 + (q + 1))
                        down(U_FFN + 16 + 4 * cg + q, c * 32, banks, 2 * q, z_hi, z_lo,
                             CHUNK // P - 1)

            chunk(0)
            with pe.Fori(1, NCHUNK) as c:
                chunk(c)

        @block.scalar
        def _(act):
            def slot(n, more):
                u = n + AHEAD
                if u >= UNITS:
                    return
                act.wait_ge(raw_landed[u % RING], (u // RING + 1) * 16 + more * 4)
                if u >= RING:
                    act.wait_ge(unit_used, u - RING + 1 + more)
                nc.scalar.copy(w_hi[:, u % RING, :], w_raw[:, u % RING, :]).then_inc(hi_ready, 1)

            for t in range(TT):
                act.dma_start(x_sb[:, t, :], xp_v[:, t, :] if t < 2 else xs_v).then_inc(x_landed[t], 16)
            slot(-2, 0)
            slot(-1, 0)
            for t in range(TT):
                act.wait_ge(x_landed[t], 16)
                nc.scalar.activation(junk0[:, :], x_sb[:, t, :], ACT.Square,
                                     accum_out=ssq[:, 0, t, 0:1]).then_inc(ssq_ready[0], 1)
                act.wait_ge(var_ready[0], t + 1)
                nc.scalar.activation(std[:, 0, t:t + 1], var[:, 0, t:t + 1], ACT.Sqrt).then_inc(std_ready[0], 1)
            act.wait_ge(gain_ready, 1)
            for k in range(KD):
                act.wait_ge(ht_psum, k + 1)
                nc.scalar.activation(ht_hi[:, k, :], ps[:, 2 + k % 6, 0:T], ACT.Copy,
                                     scale=g_pre_t[:, k:k + 1]).then_inc(ht_hi_ready, 1)

            slot(U_F, 0)
            slot(U_F + 1, 0)
            act.wait_ge(f_dve, 3)
            nc.scalar.activation(f_exp[:, :], f_abs[:, :], ACT.Exp, scale=-1.0).then_inc(f_act, 1)
            act.wait_ge(f_dve, 4)
            nc.scalar.activation(f_log[:, :], f_one[:, :], ACT.Ln).then_inc(f_act, 1)

            def pool_hi(g):
                act.wait_ge(pooled_ready, g + 1)
                nc.scalar.copy(pl_hi[:, 2 * g:2 * g + 2, :], pooled[:, :, :]).then_inc(pl_hi_ready, 1)

            for g in range(GROUPS):
                for q in range(4):
                    slot(U_U + 4 * g + q, 0)
                    if q == 2 and g >= 1:
                        pool_hi(g - 1)
                act.wait_ge(unit_used, U_U + 4 * g + 4)
                b = 4 + 2 * (g % 2)
                nc.scalar.copy(u_p[:, 2 * g:2 * g + 2, HIST:HIST + SEQ], ps[:, b:b + 2, 0:SEQ]).then_inc(u_saved, 1)
                nc.scalar.copy(u_new[:, 2 * g:2 * g + 2, :], ps[:, b:b + 2, SEQ:T])
                for c in range(2):
                    last = nc.scalar.copy(u_s[:, 2 * g + c, :, HIST:HIST + QS],
                                          ps[:, b + c, SEQ:T].rearrange("p (b q) -> p b q", q=QS))
                last.then_inc(u_saved, 1)
            for g in range(GROUPS):
                slot(U_POOL + g, 0)
                if g == 2:
                    pool_hi(GROUPS - 1)
                for j in range(2):
                    act.wait_ge(brb_psum, 3 * g + j + 1)
                    nc.scalar.activation(brb[:, 4 * g + j, :], ps[:, j, 0:T], ACT.Copy,
                                         scale=pscale_t[:, 4 * g + j:4 * g + j + 1]).then_inc(brb_act, 1)

            def values_back(a):
                act.wait_ge(tp_full[1], a * 5 + 1)
                if later(a):
                    act.wait_ge(v_stored, a * 32)
                nc.scalar.copy(v_nat[:, :, :].rearrange("p t c -> p (t c)"),
                               ps[:, TP[1], 0:T]).then_inc(tp_free[1], 1)

            def exp_prompt(a):
                act.wait_ge(nmx_ready, a * 3 + 1)
                for qt, c0, c1 in ((0, 0, P), (1, P, P + SEQ)):
                    for h in range(2):
                        e = 2 * qt + h
                        nc.scalar.activation(s_p[:, h, c0:c1], s_p[:, h, c0:c1], ACT.Exp,
                                             bias=nmx[:, e:e + 1],
                                             accum_out=esum[:, e:e + 1]).then_inc(exp_ready, 1)

            def exp_sample(a, half):
                act.wait_ge(nmx_ready, a * 3 + 2 + half)
                e = 4 + half
                nc.scalar.activation(s_s[:, half, :], s_s[:, half, :], ACT.Exp, bias=nmx[:, e:e + 1],
                                     accum_out=esum[:, e:e + 1]).then_inc(exp_ready, 1)

            def keys_in(a, half):
                act.wait_ge(tp_full[1], a * 5 + 2 + half)
                nc.scalar.copy(kts[:, 2:4, :].rearrange("p b s -> p (b s)"),
                               ps[:, TP[1], :]).then_inc(tp_free[1], 1)

            def turned_prompt(a):
                act.wait_ge(tp_full[1], a * 5 + 4)
                nc.scalar.copy(pt_p[:, 1, :], ps[:, TP[1], 0:P + SEQ]).then_inc(tp_free[1], 1)

            def turned_sample(a):
                act.wait_ge(tp_full[1], a * 5 + 5)
                nc.scalar.copy(pt_s[:, 1, :], ps[:, TP[1], 0:SCOL]).then_inc(tp_free[1], 1)

            def out_prompt(a):
                act.wait_ge(s_full[0], a * 2 + 2)
                nc.scalar.copy(at_hi[:, bass.ds(a, 1), 0:SEQ], ps[:, S[0]:S[0] + 1, 0:SEQ]).then_inc(a_hi_ready, 1)

            def out_rows(a):
                act.wait_ge(s_full[1], a * 2 + 2)
                act.wait_ge(srec_ready, a + 1)
                for half in range(2):
                    last = nc.scalar.activation(o_nat[:, half, :], ps[:, S[1], half * P:(half + 1) * P],
                                                ACT.Copy, scale=erec[:, 4 + half:5 + half])
                last.then_inc(onat_ready, 1)

            def out_sample(a):
                act.wait_ge(s_full[2], a * 2 + 2)
                for h in range(2):
                    rows = slice(HD * h, HD * (h + 1))
                    src = ps[rows, S[2], 0:2 * P].rearrange("p (b h q) -> p b h q", h=2, q=QS)[:, :, h, :]
                    dst = at_hi[rows, bass.ds(a, 1), SEQ:T].rearrange("p o (b q) -> p (o b) q", q=QS)
                    last = nc.scalar.copy(dst, src)
                last.then_inc(a_hi_ready, 1)

            def queries(hp, par):
                act.wait_ge(unit_used, hp * 6 + (U_HP + 2))
                act.wait_ge(q_zero, 1)
                bank = G[par]
                for h in range(2):
                    rows = slice(HD * h, HD * (h + 1))
                    nc.scalar.mul(qp[par][rows, h, :], ps[rows, bank, 0:SEQ], SCALE)
                    last = nc.scalar.mul(qs[par][rows, :, h, :],
                                         ps[rows, bank, SEQ:T].rearrange("p (b q) -> p b q", q=QS), SCALE)
                last.then_inc(q_saved, 1)

            def values(hp, par):
                act.wait_ge(unit_used, hp * 6 + (U_HP + 6))
                nc.scalar.copy(vt[:, :], ps[:, G[par], 0:T]).then_inc(v_saved, 1)

            def head_pair(n, more, hp, par, attend):
                a = hp - 1
                slot(n, more)
                if attend:
                    values_back(a)
                    exp_prompt(a)
                slot(n + 1, more)
                queries(hp, par)
                if attend:
                    keys_in(a, 0)
                slot(n + 2, more)
                if attend:
                    exp_sample(a, 0)
                    keys_in(a, 1)
                slot(n + 3, more)
                if attend:
                    exp_sample(a, 1)
                    turned_prompt(a)
                slot(n + 4, more)
                if attend:
                    turned_sample(a)
                slot(n + 5, more)
                if attend:
                    out_prompt(a)
                    out_rows(a)
                values(hp, par)
                if attend:
                    out_sample(a)

            head_pair(U_HP, 0, 0, 0, False)
            act.wait_ge(pool_stored, 144)
            act.wait_ge(nc_stored, 144)
            head_pair(U_HP + 6, 0, 1, 1, True)
            with act.Fori(0, 3) as i:
                for j in range(2):
                    head_pair(U_HP + 12 + 6 * j, i * 12, i * 2 + (2 + j), j, True)

            def sigmoid_a(jp):
                act.wait_ge(unit_used, jp * 10 + (U_GATE + 4))
                if later(jp):
                    act.wait_ge(m_lo_ready, jp)
                nc.scalar.activation(sg_a[:, :, :], ps[:, 0:2, 0:T], ACT.Sigmoid).then_inc(ga_ready, 1)

            def sigmoid_b(jp):
                act.wait_ge(unit_used, jp * 10 + (U_GATE + 8))
                nc.scalar.activation(sg_b[:, :, :], ps[:, 2:4, 0:T], ACT.Sigmoid).then_inc(gb_ready, 1)

            def merged_hi(jp):
                act.wait_ge(m_ready, jp + 1)
                nc.scalar.copy(mt_hi[:, bass.ds(jp * 2, 2), :], sg_a[:, :, :]).then_inc(m_hi_ready, 1)

            def gate_pair(n, more, jp):
                slot(n, more)
                slot(n + 1, more)
                merged_hi(jp - 1)
                slot(n + 2, more)
                slot(n + 3, more)
                sigmoid_a(jp)
                for q in range(4, 8):
                    slot(n + q, more)
                sigmoid_b(jp)
                slot(n + 8, more)
                slot(n + 9, more)

            slot(U_GATE, 0)
            values_back(7)
            exp_prompt(7)
            slot(U_GATE + 1, 0)
            keys_in(7, 0)
            slot(U_GATE + 2, 0)
            exp_sample(7, 0)
            keys_in(7, 1)
            slot(U_GATE + 3, 0)
            exp_sample(7, 1)
            turned_prompt(7)
            turned_sample(7)
            out_prompt(7)
            out_rows(7)
            out_sample(7)
            sigmoid_a(0)
            for q in range(4, 8):
                slot(U_GATE + q, 0)
            sigmoid_b(0)
            slot(U_GATE + 8, 0)
            slot(U_GATE + 9, 0)
            act.wait_ge(k_stored, 256)
            act.wait_ge(v_stored, 256)
            gate_pair(U_GATE + 10, 0, 1)
            with act.Fori(0, 3) as i:
                for j in range(2):
                    gate_pair(U_GATE + 20 + 10 * j, i * 20, i * 2 + (2 + j))
            merged_hi(7)

            act.sem_inc(ssq_ready[1], 1)
            with act.Fori(0, 2) as i:
                for j in range(2):
                    for q in range(8):
                        slot(U_OUT + 8 * j + q, i * 16)
                    for t in range(TT):
                        act.wait_ge(y_saved, i * 6 + (3 * j + t + 1))
                        act.wait_ge(ssq_ready[1], i * 6 + (3 * j + t + 1))
                        nc.scalar.activation(
                            junk[:, :], ybuf[:, t, bass.ds(i * 1024 + 512 * j, 512)], ACT.Square,
                            accum_out=ssq[:, 1, t, bass.ds(i * 2 + j, 1)]).then_inc(ssq_ready[1], 1)
            act.wait_ge(var_ready[1], 1)
            nc.scalar.activation(std[:, 1, :], var[:, 1, :], ACT.Sqrt).then_inc(std_ready[1], 1)

            def square2(t):
                act.wait_ge(x2_ready, t + 1)
                nc.scalar.activation(junk2[:, :], xres[:, t, :], ACT.Square,
                                     accum_out=ssq[:, 2, t, 0:1]).then_inc(ssq_ready[2], 1)
                act.wait_ge(var_ready[2], t + 1)
                nc.scalar.activation(std[:, 2, t:t + 1], var[:, 2, t:t + 1], ACT.Sqrt).then_inc(std_ready[2], 1)

            def h2_hi(t):
                for n in range(4):
                    use = 4 * t + n
                    act.wait_ge(h2_psum, use + 1)
                    bank = [6, 7, 0, 1, 2, 3][use % 6]
                    nc.scalar.copy(ht_hi[:, 4 * n:4 * n + 4, t * P:(t + 1) * P],
                                   ps[:, bank, :].rearrange("p (c q) -> p c q", q=P)).then_inc(h2_hi_ready, 1)

            square2(0)
            square2(1)
            h2_hi(0)
            square2(2)
            h2_hi(1)
            h2_hi(2)

            def chunk(n, more, c):
                for pr in range(4):
                    for q in range(4):
                        slot(n + 4 * pr + q, more)
                    act.wait_ge(unit_used, c * 32 + (U_FFN + 4 * pr + 4))
                    if pr > 0 or later(c):
                        act.wait_ge(sq_ready, c * 4 + pr)
                    b = 2 - 2 * (pr % 2)
                    nc.scalar.activation(z_relu[:, :, :], ps[:, b:b + 2, 0:T], ACT.Relu).then_inc(relu_ready, 1)
                    act.wait_ge(sq_ready, c * 4 + (pr + 1))
                    nc.scalar.copy(z_hi[:, 2 * pr:2 * pr + 2, :], z_sq[:, :, :]).then_inc(z_hi_ready, 1)
                for q in range(16):
                    slot(n + 16 + q, more)

            chunk(U_FFN, 0, 0)
            with act.Fori(1, NCHUNK - 1) as c:
                chunk(U_FFN, c * 32, c)
            chunk(U_FFN + 32 * (NCHUNK - 1), 0, NCHUNK - 1)

            for t in range(TT):
                act.wait_ge(o_added, 12 * NCHUNK - 2 + t)
                nc.scalar.activation(g_fpre_r[:, :], ybuf[:, t, :], ACT.Square,
                                     accum_out=ssq[:, 3, t, 0:1]).then_inc(ssq_ready[3], 1)
                act.wait_ge(var_ready[3], t + 1)
                nc.scalar.activation(std[:, 3, t:t + 1], var[:, 3, t:t + 1], ACT.Sqrt).then_inc(std_ready[3], 1)

        @block.vector
        def _(dve):
            def slot(n, more):
                u = n + AHEAD
                if u >= UNITS:
                    return
                dve.wait_ge(hi_ready, u + 1 + more)
                nc.vector.tensor_tensor(w_lo[:, u % RING, :], w_raw[:, u % RING, :],
                                        f32(w_hi[:, u % RING, :]), ALU.subtract).then_inc(lo_ready, 1)

            def norm_tile(m, t):
                dve.wait_ge(ssq_ready[m], t + 1)
                nc.vector.tensor_scalar(var[:, m, t:t + 1], ssq[:, m, t, 0:1], 1.0 / D, EPS,
                                        ALU.mult, ALU.add).then_inc(var_ready[m], 1)
                dve.wait_ge(std_ready[m], t + 1)
                nc.vector.reciprocal(rstd[:, m, t:t + 1], std[:, m, t:t + 1]).then_inc(rstd_ready[m], 1)
                dve.wait_ge(rstd_ready[m], t + 1)

            slot(-2, 0)
            slot(-1, 0)
            nc.vector.memset(ones[:, :], 1.0).then_inc(dve_const, 1)
            dve.wait_ge(pool_const, 3)
            nc.vector.tensor_scalar(row_i[:, 1:2], row_i[:, 0:1], 5, 4, ALU.logical_shift_right,
                                    ALU.logical_shift_left).then_inc(dve_const, 1)
            nc.vector.tensor_scalar(row_i[:, 2:3], row_i[:, 0:1], 15, None, ALU.bitwise_and).then_inc(dve_const, 1)
            dve.wait_ge(dve_const, 3)
            nc.vector.tensor_copy(row_f[:, 0:2], row_i[:, 1:3]).then_inc(dve_const, 1)
            dve.wait_ge(dve_const, 4)
            nc.vector.tensor_scalar(col_f[:, :], col_f[:, :], row_f[:, 0:1], None, ALU.subtract).then_inc(dve_const, 1)
            dve.wait_ge(dve_const, 5)
            for half in range(2):
                off = 64.0 * half
                nc.vector.tensor_scalar(mask_t[:, half, :], col_f[:, :], off, row_f[:, 1:2],
                                        ALU.subtract, ALU.is_gt).then_inc(dve_const, 1)
                nc.vector.tensor_scalar(mask_new[:, half, :], col_f[:, :], off, 0.0,
                                        ALU.subtract, ALU.is_lt).then_inc(dve_const, 1)
            dve.wait_ge(dve_const, 9)
            nc.vector.tensor_tensor(mask_t[:, :, :], mask_t[:, :, :], mask_new[:, :, :], ALU.add).then_inc(dve_const, 1)
            dve.wait_ge(dve_const, 10)
            nc.vector.tensor_scalar(mask_new[:, :, :], mask_t[:, :, :], MASKED, None, ALU.mult).then_inc(dve_const, 1)
            for g in range(GROUPS):
                for c in range(2):
                    nc.vector.tensor_scalar(recip_cnt[:, g, c, :], cnt_f[:, :], float(2 << g), None,
                                            ALU.min).then_inc(dve_const, 1)
            dve.wait_ge(dve_const, 19)
            nc.vector.reciprocal(recip_cnt[:, :, :, :].rearrange("p g c t -> p (g c t)"),
                                 recip_cnt[:, :, :, :].rearrange("p g c t -> p (g c t)")).then_inc(dve_const, 1)

            for t in range(TT):
                norm_tile(0, t)
                nc.vector.tensor_scalar(x_sb[:, t, :], x_sb[:, t, :], rstd[:, 0, t:t + 1], None,
                                        ALU.mult).then_inc(xn_ready, 1)
            dve.wait_ge(gain_psum, 1)
            nc.vector.tensor_copy(gains_t[:, :, :].rearrange("p n k -> p (n k)"), ps[:, 0, 0:2 * KD]).then_inc(gain_ready, 1)
            dve.wait_ge(gain_ready, 1)
            for k in range(KD):
                dve.wait_ge(ht_hi_ready, k + 1)
                nc.vector.scalar_tensor_tensor(out=ht_lo[:, k, :], in0=ps[:, 2 + k % 6, 0:T],
                                               scalar=g_pre_t[:, k:k + 1], in1=f32(ht_hi[:, k, :]),
                                               op0=ALU.mult, op1=ALU.subtract).then_inc(ht_lo_ready, 1)
            for n in range(2):
                dve.wait_ge(aux_psum, n + 1)
                src = ps[:, 6 + n, :].rearrange("p (c x) -> p c x", c=4)[:, :, 0:BD * HIST]
                for c in range(4):
                    last = nc.vector.tensor_copy(u_s[:, 4 * n + c, :, 0:HIST],
                                                 src[:, c, :].rearrange("p (b j) -> p b j", j=HIST))
                last.then_inc(aux_saved, 1)
            dve.wait_ge(aux_psum, 3)
            nc.vector.tensor_copy(logf_all[:, 0:PAST], ps[:, 2, 0:PAST]).then_inc(aux_saved, 1)

            slot(U_F, 0)
            slot(U_F + 1, 0)
            dve.wait_ge(unit_used, U_F + 2)
            dve.wait_ge(small_landed, 48)
            steps = [0]

            def f_step(ins):
                steps[0] += 1
                ins.then_inc(f_dve, 1)
                dve.wait_ge(f_dve, steps[0])

            f_step(nc.vector.tensor_scalar(f_x[:, :], ps[0:H, 0, 0:T], bf_t[:, 0:1], None, ALU.add))
            f_step(nc.vector.tensor_scalar(f_neg[:, :], f_x[:, :], 0.0, None, ALU.min))
            f_step(nc.vector.scalar_tensor_tensor(out=f_abs[:, :], in0=f_x[:, :], scalar=-1.0, in1=f_x[:, :],
                                                  op0=ALU.mult, op1=ALU.max))
            dve.wait_ge(f_act, 1)
            f_step(nc.vector.tensor_scalar(f_one[:, :], f_exp[:, :], 1.0, None, ALU.add))
            f_step(nc.vector.tensor_scalar(f_x[:, :], f_one[:, :], 1.0, None, ALU.subtract))
            f_step(nc.vector.tensor_scalar(f_abs[:, :], f_x[:, :], 1e-9, None, ALU.max))
            f_step(nc.vector.reciprocal(f_abs[:, :], f_abs[:, :]))
            f_step(nc.vector.tensor_tensor(f_abs[:, :], f_abs[:, :], f_exp[:, :], ALU.mult))
            dve.wait_ge(f_act, 2)
            f_step(nc.vector.tensor_tensor(f_abs[:, :], f_abs[:, :], f_log[:, :], ALU.mult))
            f_step(nc.vector.scalar_tensor_tensor(out=f_log[:, :], in0=f_x[:, :], scalar=0.0, in1=f_exp[:, :],
                                                  op0=ALU.is_equal, op1=ALU.mult))
            f_step(nc.vector.tensor_tensor(f_abs[:, :], f_abs[:, :], f_log[:, :], ALU.add))
            f_step(nc.vector.tensor_tensor(logf_t[:, :], f_neg[:, :], f_abs[:, :], ALU.subtract))
            nc.vector.tensor_tensor_scan(ncp[:, :], ones[0:H, 0:SEQ], logf_t[:, 0:SEQ], 0.0,
                                         ALU.mult, ALU.subtract).then_inc(ncp_ready, 1)

            def pool_lo(g):
                w = 2 << g
                fin = g % 2
                dve.wait_ge(win_level, (g + 1) * (g + 2) // 2)
                dve.wait_ge(u_saved, 2 * g + 2)
                if g >= 1:
                    dve.wait_ge(pl_hi_ready, g)
                    dve.wait_ge(pl_lo_ready, g)
                for c in range(2):
                    nc.vector.scalar_tensor_tensor(
                        out=pooled[:, c, HIST:SEQ], in0=win_p[:, fin, c, 2 * HIST:HIST + SEQ], scalar=1.0 / w,
                        in1=u_p[:, 2 * g + c, 2 * HIST:HIST + SEQ], op0=ALU.mult, op1=ALU.subtract)
                    nc.vector.scalar_tensor_tensor(
                        out=pooled[:, c, SEQ:T].rearrange("p (b q) -> p b q", q=QS),
                        in0=win_s[:, fin, c, :, HIST:HIST + QS], scalar=1.0 / w,
                        in1=u_s[:, 2 * g + c, :, HIST:HIST + QS], op0=ALU.mult, op1=ALU.subtract)
                nc.vector.tensor_tensor(first[:, g, :, :], win_p[:, fin, :, HIST:2 * HIST],
                                        recip_cnt[:, g, :, :], ALU.mult).then_inc(win_step, 1)
                dve.wait_ge(win_step, g + 1)
                nc.vector.tensor_tensor(pooled[:, :, 0:HIST], first[:, g, :, :],
                                        u_p[:, 2 * g:2 * g + 2, HIST:2 * HIST],
                                        ALU.subtract).then_inc(pooled_ready, 1)
                dve.wait_ge(pl_hi_ready, g + 1)
                nc.vector.tensor_tensor(pl_lo[:, 2 * g:2 * g + 2, :], pooled[:, :, :],
                                        f32(pl_hi[:, 2 * g:2 * g + 2, :]), ALU.subtract).then_inc(pl_lo_ready, 1)

            for g in range(GROUPS):
                for q in range(4):
                    slot(U_U + 4 * g + q, 0)
                    if g == 0 and q == 2:
                        dve.wait_ge(logf_new_in, 128)
                        nc.vector.tensor_tensor_scan(ncs[:, 0:PAST + QS], ones[:, :], logf_all[:, :], 0.0,
                                                     ALU.mult, ALU.subtract).then_inc(ncs_ready, 1)
                        dve.wait_ge(ncs_ready, 1)
                        for b in range(1, BD):
                            last = nc.vector.tensor_copy(ncs[:, PAST + QS * b:PAST + QS * (b + 1)],
                                                         ncs[:, PAST:PAST + QS])
                        last.then_inc(ncs_ready, 1)
                    if q == 2 and g >= 1:
                        pool_lo(g - 1)
                if g == 1:
                    dve.wait_ge(fnat_psum, 1)
                    nc.vector.tensor_copy(logf_nat[:, :, :].rearrange("p t h -> p (t h)"),
                                          ps[:, 3, 0:TT * H]).then_inc(fnat_saved, 1)
            for g in range(GROUPS):
                slot(U_POOL + g, 0)
                if g == 2:
                    pool_lo(GROUPS - 1)
                for j in range(2, 4):
                    if j == 2:
                        dve.wait_ge(brb_psum, 3 * g + 3)
                    else:
                        dve.wait_ge(unit_used, U_POOL + g + 1)
                    nc.vector.tensor_scalar(brb[:, 4 * g + j, :], ps[:, j, 0:T], pscale_t[:, 4 * g + j:4 * g + j + 1],
                                            None, ALU.mult).then_inc(brb_dve, 1)
                if g == 1:
                    for n in range(2):
                        dve.wait_ge(unat_psum, n + 1)
                        nc.vector.tensor_copy(un_p[:, 512 * n:512 * n + 512], ps[0:QS, 4 + n, :]).then_inc(unat_saved, 1)
                    for n in range(2):
                        dve.wait_ge(unat_psum, n + 3)
                        nc.vector.tensor_copy(u_nat[:, 512 * n:512 * n + 512], ps[:, 6 + n, :]).then_inc(unat_saved, 1)

            def keys_back(a):
                dve.wait_ge(tp_full[0], a * 5 + 1)
                if later(a):
                    dve.wait_ge(k_stored, a * 32)
                nc.vector.tensor_copy(k_nat[:, :, :].rearrange("p t c -> p (t c)"),
                                      ps[:, TP[0], 0:T]).then_inc(tp_free[0], 1)

            def biased(out, psum, bias, e):
                nc.vector.tensor_tensor_reduce(out, psum, bias, 1.0, LOWEST, ALU.add, ALU.max,
                                               mx[:, e:e + 1]).then_inc(max_ready, 1)

            def bias_prompt(a):
                for qt in range(2):
                    if qt == 0:
                        dve.wait_ge(bias_ready, a * 3 + 2)
                    dve.wait_ge(s_full[qt], a * 2 + 1)
                    dve.sem_inc(dve_waited, 1)
                    for h in range(2):
                        if qt == 0:
                            biased(s_p[:, h, 0:P], ps[:, S[0], h * P:(h + 1) * P], bias_0[:, h, :], h)
                        else:
                            biased(s_p[:, h, P:P + SEQ], ps[:, S[1], h * SEQ:(h + 1) * SEQ], bias_p[:, h, :],
                                   2 + h)
                dve.wait_ge(max_ready, a * 6 + 4)
                nc.vector.tensor_scalar(nmx[:, 0:4], mx[:, 0:4], -1.0, None, ALU.mult).then_inc(nmx_ready, 1)

            def bias_sample(a, half):
                if half == 0:
                    dve.wait_ge(bias_ready, a * 3 + 3)
                    dve.wait_ge(s_full[2], a * 2 + 1)
                else:
                    dve.wait_ge(s_full[3], a + 1)
                dve.sem_inc(dve_waited, 1)
                biased(s_s[:, half, :], ps[:, S[2 + half], 0:SCOL], bias_s[:, half, :], 4 + half)
                dve.wait_ge(max_ready, a * 6 + 5 + half)
                nc.vector.tensor_scalar(nmx[:, 4 + half:5 + half], mx[:, 4 + half:5 + half], -1.0, None,
                                        ALU.mult).then_inc(nmx_ready, 1)

            def keys_in(a, half):
                dve.wait_ge(tp_full[0], a * 5 + 2 + half)
                nc.vector.tensor_copy(kts[:, 0:2, :].rearrange("p b s -> p (b s)"),
                                      ps[:, TP[0], :]).then_inc(tp_free[0], 1)

            def normalise_prompt(a):
                dve.wait_ge(exp_ready, a * 6 + 4)
                nc.vector.reciprocal(erec[:, 0:4], esum[:, 0:4]).then_inc(erec_ready, 1)
                dve.wait_ge(erec_ready, a + 1)
                for e in range(4):
                    c = slice(0, P) if e < 2 else slice(P, P + SEQ)
                    last = nc.vector.tensor_scalar(s_p[:, e % 2, c], s_p[:, e % 2, c], erec[:, e:e + 1], None,
                                                   ALU.mult)
                last.then_inc(prob_ready, 1)

            def turned_prompt(a):
                dve.wait_ge(tp_full[0], a * 5 + 4)
                nc.vector.tensor_copy(pt_p[:, 0, :], ps[:, TP[0], 0:P + SEQ]).then_inc(tp_free[0], 1)

            def turned_sample(a):
                dve.wait_ge(tp_full[0], a * 5 + 5)
                nc.vector.tensor_copy(pt_s[:, 0, :], ps[:, TP[0], 0:SCOL]).then_inc(tp_free[0], 1)

            def recip_sample(a):
                dve.wait_ge(exp_ready, a * 6 + 6)
                nc.vector.reciprocal(erec[:, 4:6], esum[:, 4:6]).then_inc(srec_ready, 1)

            def out_prompt(a):
                dve.wait_ge(a_hi_ready, a * 2 + 1)
                nc.vector.tensor_tensor(at_lo[:, bass.ds(a, 1), 0:SEQ], ps[:, S[0]:S[0] + 1, 0:SEQ],
                                        f32(at_hi[:, bass.ds(a, 1), 0:SEQ]), ALU.subtract).then_inc(a_lo_ready, 1)

            def out_sample(a):
                dve.wait_ge(a_hi_ready, a * 2 + 2)
                for h in range(2):
                    rows = slice(HD * h, HD * (h + 1))
                    src = ps[rows, S[2], 0:2 * P].rearrange("p (b h q) -> p b h q", h=2, q=QS)[:, :, h, :]
                    hi = at_hi[rows, bass.ds(a, 1), SEQ:T].rearrange("p o (b q) -> p (o b) q", q=QS)
                    lo = at_lo[rows, bass.ds(a, 1), SEQ:T].rearrange("p o (b q) -> p (o b) q", q=QS)
                    last = nc.vector.tensor_tensor(lo, src, f32(hi), ALU.subtract)
                last.then_inc(a_lo_ready, 1)

            def keys(hp, par):
                dve.wait_ge(unit_used, hp * 6 + (U_HP + 4))
                dve.wait_ge(q_zero, 1)
                nc.vector.tensor_copy(kt[par][:, :], ps[:, G[1 - par], 0:T]).then_inc(k_saved, 1)

            def head_pair(n, more, hp, par, attend):
                a = hp - 1
                slot(n, more)
                if attend:
                    keys_back(a)
                    bias_prompt(a)
                slot(n + 1, more)
                if attend:
                    keys_in(a, 0)
                    normalise_prompt(a)
                slot(n + 2, more)
                if attend:
                    bias_sample(a, 0)
                    keys_in(a, 1)
                slot(n + 3, more)
                keys(hp, par)
                if attend:
                    bias_sample(a, 1)
                    turned_prompt(a)
                slot(n + 4, more)
                if attend:
                    recip_sample(a)
                    turned_sample(a)
                slot(n + 5, more)
                if attend:
                    out_prompt(a)
                    out_sample(a)

            head_pair(U_HP, 0, 0, 0, False)
            head_pair(U_HP + 6, 0, 1, 1, True)
            with dve.Fori(0, 3) as i:
                for j in range(2):
                    head_pair(U_HP + 12 + 6 * j, i * 12, i * 2 + (2 + j), j, True)

            def gated_a(jp):
                dve.wait_ge(unit_used, jp * 10 + (U_GATE + 10))
                dve.wait_ge(ga_ready, jp + 1)
                nc.vector.tensor_tensor(sg_a[:, :, :], ps[:, 4:6, 0:T], sg_a[:, :, :], ALU.mult).then_inc(ta_ready, 1)

            def merged_lo(jp):
                dve.wait_ge(m_hi_ready, jp + 1)
                nc.vector.tensor_tensor(mt_lo[:, bass.ds(jp * 2, 2), :], sg_a[:, :, :],
                                        f32(mt_hi[:, bass.ds(jp * 2, 2), :]), ALU.subtract).then_inc(m_lo_ready, 1)

            def gate_pair(n, more, jp):
                slot(n, more)
                slot(n + 1, more)
                merged_lo(jp - 1)
                for q in range(2, 10):
                    slot(n + q, more)
                gated_a(jp)

            slot(U_GATE, 0)
            keys_back(7)
            bias_prompt(7)
            slot(U_GATE + 1, 0)
            keys_in(7, 0)
            normalise_prompt(7)
            slot(U_GATE + 2, 0)
            bias_sample(7, 0)
            keys_in(7, 1)
            slot(U_GATE + 3, 0)
            bias_sample(7, 1)
            turned_prompt(7)
            recip_sample(7)
            turned_sample(7)
            out_prompt(7)
            out_sample(7)
            for q in range(4, 10):
                slot(U_GATE + q, 0)
            gated_a(0)
            gate_pair(U_GATE + 10, 0, 1)
            with dve.Fori(0, 3) as i:
                for j in range(2):
                    gate_pair(U_GATE + 20 + 10 * j, i * 20, i * 2 + (2 + j))
            merged_lo(7)

            with dve.Fori(0, 2) as i:
                for j in range(2):
                    for q in range(8):
                        slot(U_OUT + 8 * j + q, i * 16)
                    dve.wait_ge(unit_used, i * 16 + (U_OUT + 8 * j + 8))
                    for t in range(TT):
                        nc.vector.tensor_copy(ybuf[:, t, bass.ds(i * 1024 + 512 * j, 512)],
                                              ps[:, 3 * j + t, :]).then_inc(y_saved, 1)
            dve.wait_ge(ssq_ready[1], 13)
            nc.vector.tensor_reduce(std[:, 1, :], ssq[:, 1, :, :], mybir.AxisListType.X, ALU.add).then_inc(rstd_ready[1], 1)
            dve.wait_ge(rstd_ready[1], 1)
            nc.vector.tensor_scalar(var[:, 1, :], std[:, 1, :], 1.0 / D, EPS, ALU.mult, ALU.add).then_inc(var_ready[1], 1)
            dve.wait_ge(std_ready[1], 1)
            nc.vector.reciprocal(rstd[:, 1, :], std[:, 1, :]).then_inc(rstd_ready[1], 1)
            dve.wait_ge(rstd_ready[1], 2)

            def add_mix(t):
                if t == 0:
                    dve.wait_ge(gpost_landed, 16)
                    dve.wait_ge(xres_landed, 48)
                nc.vector.scalar_tensor_tensor(out=ybuf[:, t, :], in0=ybuf[:, t, :], scalar=rstd[:, 1, t:t + 1],
                                               in1=g_post_r[:, :], op0=ALU.mult, op1=ALU.mult).then_inc(yn_ready, 1)
                dve.wait_ge(yn_ready, t + 1)
                nc.vector.tensor_tensor(xres[:, t, :], xres[:, t, :], ybuf[:, t, :], ALU.add).then_inc(x2_ready, 1)

            def norm_rows(t):
                if t == 0:
                    dve.wait_ge(gfpre_landed, 16)
                norm_tile(2, t)
                nc.vector.scalar_tensor_tensor(out=ybuf[:, t, :], in0=xres[:, t, :], scalar=rstd[:, 2, t:t + 1],
                                               in1=g_fpre_r[:, :], op0=ALU.mult, op1=ALU.mult).then_inc(hn_ready, 1)

            def h2_lo(t):
                for n in range(4):
                    use = 4 * t + n
                    dve.wait_ge(h2_hi_ready, use + 1)
                    bank = [6, 7, 0, 1, 2, 3][use % 6]
                    dst = slice(t * P, (t + 1) * P)
                    nc.vector.tensor_tensor(ht_lo[:, 4 * n:4 * n + 4, dst],
                                            ps[:, bank, :].rearrange("p (c q) -> p c q", q=P),
                                            f32(ht_hi[:, 4 * n:4 * n + 4, dst]), ALU.subtract).then_inc(h2_lo_ready, 1)

            add_mix(0)
            add_mix(1)
            norm_rows(0)
            add_mix(2)
            norm_rows(1)
            h2_lo(0)
            norm_rows(2)
            h2_lo(1)
            h2_lo(2)

            def chunk(n, more, c):
                for pr in range(4):
                    for q in range(4):
                        slot(n + 4 * pr + q, more)
                    dve.wait_ge(relu_ready, c * 4 + (pr + 1))
                    nc.vector.tensor_tensor(z_sq[:, :, :], z_relu[:, :, :], z_relu[:, :, :], ALU.mult).then_inc(sq_ready, 1)
                    dve.wait_ge(z_hi_ready, c * 4 + (pr + 1))
                    nc.vector.tensor_tensor(z_lo[:, 2 * pr:2 * pr + 2, :], z_sq[:, :, :],
                                            f32(z_hi[:, 2 * pr:2 * pr + 2, :]), ALU.subtract).then_inc(z_lo_ready, 1)
                for cg in range(4):
                    for q in range(4):
                        slot(n + 16 + 4 * cg + q, more)
                    dve.wait_ge(unit_used, c * 32 + (U_FFN + 16 + 4 * cg + 4))
                    for t in range(TT):
                        bank = [[4, 5, 6], [7, 0, 1]][cg % 2][t]
                        dst = ybuf[:, t, 512 * cg:512 * cg + 512]
                        nc.vector.tensor_tensor(dst, ps[:, bank, :], dst, ALU.add).then_inc(o_added, 1)

            dve.wait_ge(acc_zero, 1)
            with dve.Fori(0, NCHUNK - 1) as c:
                chunk(U_FFN, c * 32, c)
            chunk(U_FFN + 32 * (NCHUNK - 1), 0, NCHUNK - 1)

            dve.wait_ge(gfpost_landed, 16)
            for t in range(TT):
                norm_tile(3, t)
                nc.vector.scalar_tensor_tensor(out=ybuf[:, t, :], in0=ybuf[:, t, :], scalar=rstd[:, 3, t:t + 1],
                                               in1=g_fpost_r[:, :], op0=ALU.mult, op1=ALU.mult).then_inc(on_ready, 1)
                dve.wait_ge(on_ready, t + 1)
                nc.vector.tensor_tensor(ybuf[:, t, :], xres[:, t, :], ybuf[:, t, :], ALU.add).then_inc(out_ready, 1)

        @block.gpsimd
        def _(pool):
            pool.dma_start(gain_nat[:, 0, :], g_mix_pre.rearrange("o (k p) -> (o k) p", p=P)).then_inc(small_landed, 16)
            pool.dma_start(gain_nat[:, 1, :], pool_scale.rearrange("o (k p) -> (o k) p", p=P)).then_inc(small_landed, 16)
            pool.dma_start(bf_t[:, :], b_f.rearrange("o h -> h o"),
                           allow_slow_non_contiguous=True).then_inc(small_landed, 16)
            pool.dma_start(st_nat[:, :], state_pool.rearrange("o b j c -> (o b j) c")).then_inc(state_landed, 16)
            for t in range(BATCH_KEYS):
                pool.dma_start(clf[:, t, :].rearrange("p (b h) -> p b h", h=H), clf_v[t]).then_inc(clf_landed, 16)
            nc.gpsimd.memset(ident[:, :], 0.0).then_inc(ident_zero, 1)
            pool.wait_ge(ident_zero, 1)
            nc.gpsimd.affine_select(out=ident[:, :], in_=ident[:, :], compare_op=ALU.not_equal, fill=1.0, base=0,
                                    pattern=[[-1, P]], channel_multiplier=1).then_inc(pool_const, 1)
            nc.gpsimd.iota(row_i[:, 0:1], pattern=[[0, 1]], base=0, channel_multiplier=1).then_inc(pool_const, 1)
            nc.gpsimd.iota(cnt_f[:, :], pattern=[[1, HIST]], base=1, channel_multiplier=0,
                           allow_small_or_imprecise_dtypes=True)
            nc.gpsimd.iota(col_f[:, :], pattern=[[1, P]], base=0, channel_multiplier=0,
                           allow_small_or_imprecise_dtypes=True).then_inc(pool_const, 1)
            nc.gpsimd.memset(u_p[:, :, 0:HIST], 0.0).then_inc(pool_const, 1)

            pool.wait_ge(f_dve, 12)
            for b in range(BD):
                pool.dma_start(logf_all[H * b:H * (b + 1), PAST:PAST + QS],
                               logf_t[:, SEQ + QS * b:SEQ + QS * (b + 1)]).then_inc(logf_new_in, 16)
            pool.wait_ge(ncp_ready, 1)
            pool.dma_start(ncp_dram, ncp[:, :]).then_inc(nc_stored, 16)

            def windows(g):
                if g == 0:
                    pool.wait_ge(pool_const, 4)
                pool.wait_ge(u_saved, 2 * g + 2)
                if g >= 1:
                    pool.wait_ge(pooled_ready, g)
                for lev in range(g + 1):
                    d, lo = 1 << lev, (2 << lev) - 1
                    src_p = u_p[:, 2 * g:2 * g + 2, :] if lev == 0 else win_p[:, (lev - 1) % 2, :, :]
                    if lev >= 1:
                        pool.wait_ge(win_level, levels[0])
                    dst = lev % 2
                    nc.gpsimd.tensor_tensor(win_p[:, dst, :, lo:], src_p[:, :, lo:],
                                            src_p[:, :, lo - d:HIST + SEQ - d], ALU.add)
                    for c in range(2):
                        src_s = u_s[:, 2 * g + c, :, :] if lev == 0 else win_s[:, (lev - 1) % 2, c, :, :]
                        last = nc.gpsimd.tensor_tensor(win_s[:, dst, c, :, lo:], src_s[:, :, lo:],
                                                       src_s[:, :, lo - d:HIST + QS - d], ALU.add)
                    levels[0] += 1
                    last.then_inc(win_level, 1)

            levels = [0]
            windows(0)
            pool.wait_ge(ncs_ready, 2)
            for b in range(BD):
                pool.dma_start(ncs_dram[:, b, :, :],
                               ncs[H * b:H * (b + 1), :]).then_inc(nc_stored, 16)
            windows(1)
            pool.wait_ge(fnat_saved, 1)
            pool.dma_start(lfp_v, logf_nat[:, 0:2, :]).then_inc(logf_stored, 16)
            pool.dma_start(lfs_v, logf_nat[:, 2, :]).then_inc(logf_stored, 16)
            windows(2)
            windows(3)
            pool.wait_ge(unat_saved, 4)
            pool.dma_start(pool_prompt[0, 0], un_p[1:QS, :]).then_inc(pool_stored, 16)
            for b in range(BD):
                pool.dma_start(pool_sample[0, b], u_nat[QS * b + 1:QS * (b + 1), :]).then_inc(pool_stored, 16)

            pool.wait_ge(unit_used, U_HP)
            pool.wait_ge(pool_stored, 144)
            for n in range(2):
                nc.gpsimd.memset(qp[n][:, :, :], 0.0)
                last = nc.gpsimd.memset(qs[n][:, :, :, :], 0.0)
            last.then_inc(q_zero, 1)
            pool.wait_ge(nc_stored, 144)
            pool.wait_ge(logf_stored, 32)

            def load_keys(a):
                pool.dma_start(kc[:, :, :], ck_v[:, :, bass.ds(a * P, P)]).then_inc(kc_landed, 16)

            def load_values(a):
                pool.dma_start(vc[:, :, :], cv_v[:, :, bass.ds(a * P, P)]).then_inc(vc_landed, 16)

            def load_bias(a):
                pool.dma_start(bias_p[:, :, :],
                               ncp_dram[bass.ds(a * 2, 2), :].unsqueeze(0).broadcast_to([P, 2, SEQ])
                               ).then_inc(bias_landed, 16)
                for half in range(2):
                    for b in range(4):
                        src = ncs_dram[bass.ds(a, 1), 4 * half + b, :, :]
                        src = src.rearrange("o h n -> h o n").broadcast_to([2, QS, SCOL])
                        pool.dma_start(bias_s[32 * b:32 * b + 32, half, :], src).then_inc(bias_landed, 16)
                pool.wait_ge(bias_landed, a * 144 + 144)
                pool.sem_inc(pool_waited, 1)
                nc.gpsimd.affine_select(out=bias_0[:, :, :], in_=bias_p[:, :, 0:P], compare_op=ALU.is_ge,
                                        fill=MASKED, base=0, pattern=[[0, 2], [-1, P]],
                                        channel_multiplier=1).then_inc(bias_ready, 1)
                nc.gpsimd.affine_select(out=bias_p[:, :, P:SEQ], in_=bias_p[:, :, P:SEQ], compare_op=ALU.is_ge,
                                        fill=MASKED, base=0, pattern=[[0, 2], [-1, P]],
                                        channel_multiplier=1).then_inc(bias_ready, 1)
                nc.gpsimd.tensor_tensor(bias_s[:, :, PAST:SCOL], bias_s[:, :, PAST:SCOL], mask_new[:, :, :],
                                        ALU.add).then_inc(bias_ready, 1)

            def store_rows(a):
                cols = bass.ds(a * P, P)
                pool.wait_ge(tp_free[0], a * 5 + 1)
                pool.sem_inc(pool_waited, 1)
                pool.dma_start(kp_v[:, :, cols], k_nat[:, 0:2, :]).then_inc(k_stored, 16)
                pool.dma_start(ks_v[:, cols], k_nat[:, 2, :]).then_inc(k_stored, 16)
                pool.wait_ge(tp_free[1], a * 5 + 1)
                pool.sem_inc(pool_waited, 1)
                pool.dma_start(vp_v[:, :, cols], v_nat[:, 0:2, :]).then_inc(v_stored, 16)
                pool.dma_start(vs_v[:, cols], v_nat[:, 2, :]).then_inc(v_stored, 16)

            pool.wait_ge(dve_const, 11)
            load_keys(0)
            load_bias(0)
            load_values(0)
            with pool.Fori(0, 7) as a:
                store_rows(a)
                pool.wait_ge(tp_full[0], a * 5 + 3)
                pool.wait_ge(tp_full[1], a * 5 + 3)
                load_keys(a + 1)
                pool.wait_ge(max_ready, a * 6 + 6)
                load_bias(a + 1)
                pool.wait_ge(s_full[1], a * 2 + 2)
                pool.sem_inc(pool_waited, 1)
                load_values(a + 1)
            store_rows(7)

            with pool.Fori(0, KD // 2) as jp:
                pool.wait_ge(gb_ready, jp + 1)
                nc.gpsimd.tensor_tensor(sg_b[:, :, :], sg_b[:, :, :], brb[:, bass.ds(jp * 2, 2), :],
                                        ALU.mult).then_inc(tb_ready, 1)
                pool.wait_ge(ta_ready, jp + 1)
                pool.wait_ge(tb_ready, jp + 1)
                nc.gpsimd.tensor_tensor(sg_a[:, :, :], sg_a[:, :, :], sg_b[:, :, :], ALU.add).then_inc(m_ready, 1)

            for t in range(TT):
                pool.dma_start(xres[:, t, :], xp_v[:, t, :] if t < 2 else xs_v).then_inc(xres_landed, 16)
            pool.wait_ge(m_lo_ready, KD // 2)
            pool.dma_start(g_post_r[:, :], g_mix_post.broadcast_to([P, D])).then_inc(gpost_landed, 16)
            pool.wait_ge(unit_used, U_OUT + 32)
            pool.dma_start(g_fpre_r[:, :], g_ffn_pre.broadcast_to([P, D])).then_inc(gfpre_landed, 16)
            pool.dma_start(g_fpost_r[:, :], g_ffn_post.broadcast_to([P, D])).then_inc(gfpost_landed, 16)
            pool.wait_ge(h2_psum, 4 * TT)
            nc.gpsimd.memset(ybuf[:, :, :], 0.0).then_inc(acc_zero, 1)
            pool.wait_ge(k_stored, 256)
            pool.wait_ge(v_stored, 256)


_INS = ["x_prompt", "x_sample", "cache_k", "cache_v", "cache_logf", "state_pool", "g_mix_pre", "w_in",
        "b_f", "w_attn_up", "w_pool", "pool_scale", "w_out", "g_mix_post", "g_ffn_pre", "w_ff1", "w_ff2",
        "g_ffn_post"]
_OUTS = [(1, SEQ, D), (BD, QS, D), (1, 1, SEQ, H, HD), (1, 1, SEQ, H, HD), (1, 1, SEQ, H),
         (1, 1, HIST, POOLW), (1, BD, QS, H, HD), (1, BD, QS, H, HD), (1, BD, QS, H), (1, BD, HIST, POOLW)]


def kernel(**inputs):
    import numpy as _np
    import concourse.bacc as _bacc
    from concourse import mybir as _mybir
    from concourse.bass_utils import run_bass_kernel_spmd as _run

    nc = _bacc.Bacc("TRN2", target_bir_lowering=False, num_devices=1)
    arrays, args = {}, []
    for name in _INS:
        a = _np.ascontiguousarray(inputs[name])
        arrays[f"in_{name}_dram"] = a
        args.append(nc.dram_tensor(f"in_{name}_dram", a.shape, _mybir.dt.from_np(a.dtype),
                                   kind="ExternalInput").ap())
    for i, shape in enumerate(_OUTS):
        args.append(nc.dram_tensor(f"out_{i}_dram", shape, _mybir.dt.float32, kind="ExternalOutput").ap())
    streaming_encoder(nc, *args)
    r = _run(nc, [arrays], core_ids=[0])
    return tuple(r.results[0][f"out_{i}_dram"] for i in range(len(_OUTS)))
```

```python
from contextlib import ExitStack

import concourse.bass as bass
from concourse import mybir

F32 = mybir.dt.float32
F32R = mybir.dt.float32r
I32 = mybir.dt.int32
ALU = mybir.AluOpType
ACT = mybir.ActivationFunctionType

P = 128
D = 2048
KD = D // P
SEQ = 256
BD = 8
QS = 16
PAST = 256
T = SEQ + BD * QS
TT = T // P
H = 16
HD = 64
PAIRS = H // 2
AW = H * HD
POOLW = 1024
PC = POOLW // P
HIST = 15
GROUPS = 4
ORDER = (3, 2, 1, 0)
DFF = 4 * D
EPS = 1e-6
SCALE = HD ** -0.5
OFF_K, OFF_V, OFF_F = AW, 2 * AW, 3 * AW
OFF_U = OFF_F + H
OFF_GA = OFF_U + POOLW
OFF_GB = OFF_GA + D
MASKED = -1e30
LOWEST = -3e38

UW = 1024
RING = 4
AHEAD = 2
CHUNK = 1024
NCHUNK = DFF // CHUNK
BATCH_KEYS = PAST // P
SCOL = PAST + P

U_F = 0
U_U = U_F + 2
U_POOL = U_U + 4 * GROUPS
U_HP = U_POOL + GROUPS
U_GATE = U_HP + 6 * PAIRS
U_OUT = U_GATE + 10 * (KD // 2)
U_FFN = U_OUT + 8 * 4
UNITS = U_FFN + 32 * NCHUNK


def streaming_encoder(nc, x_prompt, x_sample, cache_k, cache_v, cache_logf, state_pool,
                      g_mix_pre, w_in, b_f, w_attn_up, w_pool, pool_scale, w_out,
                      g_mix_post, g_ffn_pre, w_ff1, w_ff2, g_ffn_post,
                      y_prompt, y_sample, k_prompt, v_prompt, logf_prompt, pool_prompt,
                      k_sample, v_sample, logf_sample, pool_sample):
    xp_v = x_prompt.rearrange("o (t p) d -> p (o t) d", p=P)
    xs_v = x_sample.rearrange("b q d -> (b q) d")
    win_v = w_in.rearrange("o (k p) n -> p (o k) n", p=P)
    wup_v = w_attn_up.rearrange("o (k p) n -> p (o k) n", p=P)
    wpool_v = w_pool.rearrange("o g (k p) n -> g p (o k) n", p=P)
    wout_v = w_out.rearrange("o (k p) n -> p (o k) n", p=P)
    wff1_v = w_ff1.rearrange("o (k p) n -> p (o k) n", p=P)
    wff2_v = w_ff2.rearrange("o (k p) n -> p (o k) n", p=P)
    ck_v = cache_k.rearrange("o b (t p) h d -> p (o b t) (h d)", p=P)
    cv_v = cache_v.rearrange("o b (t p) h d -> p (o b t) (h d)", p=P)
    clf_v = cache_logf.rearrange("o b (t p) h -> t p (o b) h", p=P)
    kp_v = k_prompt.rearrange("l o (t p) h d -> p (l o t) (h d)", p=P)
    vp_v = v_prompt.rearrange("l o (t p) h d -> p (l o t) (h d)", p=P)
    ks_v = k_sample.rearrange("l b q h d -> (l b q) (h d)")
    vs_v = v_sample.rearrange("l b q h d -> (l b q) (h d)")
    yp_v = y_prompt.rearrange("o (t p) d -> p (o t) d", p=P)
    ys_v = y_sample.rearrange("b q d -> (b q) d")
    lfp_v = logf_prompt.rearrange("l o (t p) h -> p (l o t) h", p=P)
    lfs_v = logf_sample.rearrange("l b q h -> (l b q) h")
    ncp_dram = nc.dram_tensor("ncp_dram", [H, SEQ], F32, kind="Internal").ap()
    ncs_dram = nc.dram_tensor("ncs_dram", [PAIRS, BD, 2, SCOL], F32, kind="Internal").ap()

    BASE = (nc.sbuf_base + 63) // 64 * 64
    at = [0]

    def place(name, shape, dt, offset=None):
        size = 4
        for n in shape[1:]:
            size *= n
        if offset is None:
            offset = at[0]
        at[0] = (offset + size + 31) // 32 * 32
        return nc.alloc_sbuf_tensor_at(name, shape, dt, offset=BASE + offset)

    KB = 1024
    w_raw = place("w_raw", [P, RING, UW], F32)
    w_hi = place("w_hi", [P, RING, UW], F32R)
    w_lo = place("w_lo", [P, RING, UW], F32R)
    HT = at[0]
    ht_hi = place("ht_hi", [P, KD, T], F32R)
    ht_lo = place("ht_lo", [P, KD, T], F32R)
    BRB = at[0]
    z_gain = place("z_gain", [P, TT, D], F32, HT)
    brb = place("brb", [P, KD, T], F32, BRB)
    xres = place("xres", [P, TT, D], F32, BRB)
    junk0 = place("junk0", [P, D], F32, BRB)
    u_new = place("u_new", [P, PC, BD * QS], F32, BRB)
    at[0] = BRB + 24 * 1024
    ATT = at[0]
    at_hi = place("at_hi", [P, PAIRS, T], F32R)
    at_lo = place("at_lo", [P, PAIRS, T], F32R)
    END_ATT = at[0]
    ybuf = place("ybuf", [P, TT, D], F32, ATT)
    f_x = place("f_x", [H, T], F32, ATT)
    f_neg = place("f_neg", [H, T], F32)
    f_abs = place("f_abs", [H, T], F32)
    f_exp = place("f_exp", [H, T], F32)
    f_one = place("f_one", [H, T], F32)
    f_log = place("f_log", [H, T], F32)
    logf_t = place("logf_t", [H, T], F32)
    logf_nat = place("logf_nat", [P, TT, H], F32)
    ncp = place("ncp", [H, SEQ], F32)
    clf = place("clf", [P, BATCH_KEYS, BD * H], F32)
    logf_all = place("logf_all", [P, PAST + QS], F32)
    ncs = place("ncs", [P, SCOL], F32)
    gain_nat = place("gain_nat", [KD, 3, P], F32)
    ones = place("ones", [P, PAST + QS], F32)
    u_nat = place("u_nat", [P, POOLW], F32)
    assert at[0] <= END_ATT
    ident = place("ident", [P, P], F32, END_ATT)
    gains_t = place("gains_t", [P, 3, KD], F32)
    g_pre_t, pscale_t, g_fpre_t = (gains_t[:, n, :] for n in range(3))
    mask_new = place("mask_new", [P, 2, P], F32)
    recip_cnt = place("recip_cnt", [P, GROUPS, 2, HIST], F32)
    first = place("first", [P, GROUPS, 2, HIST], F32)
    bf_t = place("bf_t", [H, 1], F32)
    ssq = place("ssq", [P, 4, TT, 4], F32)
    var = place("var", [P, 4, TT], F32)
    std = place("std", [P, 4, TT], F32)
    rstd = place("rstd", [P, 4, TT], F32)
    root_warm = place("root_warm", [P, TT], F32)
    ssq_sum = place("ssq_sum", [P, 4, TT], F32)
    factor = place("factor", [P, 4, TT], F32)
    row_i = place("row_i", [P, 3], I32)
    row_f = place("row_f", [P, 2], F32)
    col_f = place("col_f", [P, P], F32)
    cnt_f = place("cnt_f", [P, HIST], F32)
    mask_t = place("mask_t", [P, 2, P], F32)
    mx = place("mx", [P, 6], F32)
    nmx = place("nmx", [P, 6], F32)
    esum = place("esum", [P, 6], F32)
    erec = place("erec", [P, 6], F32)
    R = (at[0] + 63) // 64 * 64
    LIMIT = nc.sbuf_usable_end - BASE
    x_sb = place("x_sb", [P, TT, D], F32, R)
    pl_hi = place("pl_hi", [P, PC, T], F32R, R)
    pl_lo = place("pl_lo", [P, PC, T], F32R)
    u_p = place("u_p", [P, PC, HIST + SEQ], F32)
    u_s = place("u_s", [P, PC, BD, HIST + QS], F32)
    win_p = place("win_p", [P, 2, 2, HIST + SEQ], F32)
    win_s = place("win_s", [P, 2, 2, BD, HIST + QS], F32)
    st_nat = place("st_nat", [BD * HIST, POOLW], F32)
    pooled = place("pooled", [P, 2, T], F32, at[0] - 4 * KB)
    un_p = place("un_p", [QS, POOLW], F32)

    kc = place("kc", [P, BD * BATCH_KEYS, P], F32, R)
    vc = place("vc", [P, BD * BATCH_KEYS, P], F32)
    kts = place("kts", [P, 4, PAST], F32)
    qp = [place(f"qp{n}", [P, 2, SEQ], F32) for n in range(2)]
    qs = [place(f"qs{n}", [P, BD, 2, QS], F32) for n in range(2)]
    kt = [place(f"kt{n}", [P, T], F32) for n in range(2)]
    vt = place("vt", [P, T], F32)
    k_nat = place("k_nat", [P, TT, P], F32)
    v_nat = place("v_nat", [P, TT, P], F32)
    bias_p = place("bias_p", [P, 2, SEQ], F32)
    bias_0 = place("bias_0", [P, 2, P], F32)
    bias_s = place("bias_s", [P, 2, SCOL], F32)
    s_p = place("s_p", [P, 2, P + SEQ], F32)
    s_s = place("s_s", [P, 2, SCOL], F32)
    pt_p = place("pt_p", [P, 2, P + SEQ], F32)
    pt_s = place("pt_s", [P, 2, SCOL], F32)
    o_nat = place("o_nat", [P, 2, P], F32)
    assert at[0] <= LIMIT, (at[0], LIMIT)
    sg_a = place("sg_a", [P, 2, T], F32, R)
    sg_b = place("sg_b", [P, 2, T], F32)
    mt_hi = place("mt_hi", [P, KD, T], F32R, R + 8 * KB)
    mt_lo = place("mt_lo", [P, KD, T], F32R)
    junk = place("junk", [P, 512], F32)
    assert at[0] <= LIMIT
    g_post_r = place("g_post_r", [P, D], F32, R)
    g_fpost_r = place("g_fpost_r", [P, D], F32, R + 16 * KB)
    z_hi = place("z_hi", [P, CHUNK // P, T], F32R)
    z_lo = place("z_lo", [P, CHUNK // P, T], F32R)
    z_relu = place("z_relu", [P, 2, T], F32)
    z_sq = place("z_sq", [P, 2, T], F32)
    junk2 = place("junk2", [P, D // 2], F32, R + 24 * KB)
    junk3 = place("junk3", [P, 512], F32, R)

    with ExitStack() as ctx:
        ps = ctx.enter_context(nc.psum_tensor("ps", [P, 8, 512], F32))

        def sem(name):
            return ctx.enter_context(nc.semaphore(name))

        def sems(name, n):
            return [sem(f"{name}{i}") for i in range(n)]

        G = [0, 1]
        TP = [2, 3]
        S = [4, 5, 6, 7]

        raw_landed = sems("raw_landed", RING)
        hi_ready = sem("hi_ready")
        lo_ready = sem("lo_ready")
        unit_used = sem("unit_used")
        x_landed = sems("x_landed", TT)
        gains_landed, bf_landed = sem("gains_landed"), sem("bf_landed")
        state_landed = sem("state_landed")
        clf_landed = sem("clf_landed")
        pool_const = sem("pool_const")
        dve_const = sem("dve_const")
        sp_waited, dve_waited, pool_waited = sem("sp_waited"), sem("dve_waited"), sem("pool_waited")
        ssq_ready = sems("ssq_ready", 4)
        norm_done = sem("norm_done")
        var_ready = sems("var_ready", 4)
        std_ready = sems("std_ready", 4)
        xn_ready = sem("xn_ready")
        gain_psum, gain_ready = sem("gain_psum"), sem("gain_ready")
        ht_psum = sem("ht_psum")
        ht_hi_ready = sem("ht_hi_ready")
        ht_lo_ready = sem("ht_lo_ready")
        aux_psum = sem("aux_psum")
        hist_saved, aux_saved = sem("hist_saved"), sem("aux_saved")
        f_dve = sem("f_dve")
        f_act = sem("f_act")
        fnat_psum = sem("fnat_psum")
        fnat_saved = sem("fnat_saved")
        logf_new_in = sem("logf_new_in")
        ncp_ready = sem("ncp_ready")
        ncs_ready = sem("ncs_ready")
        nc_stored = sem("nc_stored")
        u_saved = sem("u_saved")
        win_level = sem("win_level")
        ident_zero = sem("ident_zero")
        win_step = sem("win_step")
        pooled_ready = sem("pooled_ready")
        pl_hi_ready = sem("pl_hi_ready")
        pl_lo_ready = sem("pl_lo_ready")
        brb_psum = sem("brb_psum")
        brb_act = sem("brb_act")
        brb_dve = sem("brb_dve")
        unat_psum = sem("unat_psum")
        unat_saved = sem("unat_saved")
        q_saved, k_saved, v_saved = sem("q_saved"), sem("k_saved"), sem("v_saved")
        q_zero = sem("q_zero")
        tp_full = sems("tp_full", 2)
        tp_free = sems("tp_free", 2)
        s_full = sems("s_full", 4)
        kc_landed, vc_landed = sem("kc_landed"), sem("vc_landed")
        bias_landed = sem("bias_landed")
        bias_ready = sem("bias_ready")
        max_ready = sem("max_ready")
        nmx_ready = sem("nmx_ready")
        exp_ready = sem("exp_ready")
        erec_ready = sem("erec_ready")
        prob_ready = sem("prob_ready")
        srec_ready = sem("srec_ready")
        onat_ready = sem("onat_ready")
        k_stored, v_stored = sem("k_stored"), sem("v_stored")
        a_hi_ready, a_lo_ready = sem("a_hi_ready"), sem("a_lo_ready")
        ga_ready, gb_ready = sem("ga_ready"), sem("gb_ready")
        ta_ready, tb_ready = sem("ta_ready"), sem("tb_ready")
        m_ready = sem("m_ready")
        m_hi_ready, m_lo_ready = sem("m_hi_ready"), sem("m_lo_ready")
        y_saved = sem("y_saved")
        xres_landed = sem("xres_landed")
        gpost_landed = sem("gpost_landed")
        gfpost_landed = sem("gfpost_landed")
        y_psum = sem("y_psum")
        x2_ready = sem("x2_ready")
        hn_ready, hn1_ready = sem("hn_ready"), sem("hn1_ready")
        h2_psum = sem("h2_psum")
        h2_hi_ready, h2_lo_ready = sem("h2_hi_ready"), sem("h2_lo_ready")
        acc_zero = sem("acc_zero")
        relu_ready = sem("relu_ready")
        sq_ready = sem("sq_ready")
        z_hi_ready, z_lo_ready = sem("z_hi_ready"), sem("z_lo_ready")
        o_psum = sem("o_psum")
        o_added = sem("o_added")
        o_gained = sem("o_gained")
        out_ready = sem("out_ready")
        pool_stored, logf_stored = sem("pool_stored"), sem("logf_stored")
        stored = sem("stored")

        block = ctx.enter_context(nc.Block())

        def f32(ap):
            return ap.bitcast(F32)

        def later(index):
            return not isinstance(index, int) or index > 0

        @block.sync
        def _(sp):
            def load(n, more, src, k, w, apart=False):
                slot = n % RING
                if n >= RING:
                    sp.wait_ge(lo_ready, n - RING + 1 + more)
                    if apart:
                        sp.sem_inc(sp_waited, 1)
                dst = w_raw[:, slot, :].rearrange("p (k w) -> p k w", w=w)
                sp.dma_start(dst, src).then_inc(raw_landed[slot], 16)

            def win(k0, nk, c0, w):
                return win_v[:, k0:k0 + nk, bass.ds(c0, w)]

            for t in range(TT):
                sp.dma_start(x_sb[:, t, :], xp_v[:, t, :] if t < 2 else xs_v).then_inc(x_landed[t], 16)
            sp.dma_start(gain_nat[:, 0, :], g_mix_pre.rearrange("o (k p) -> (o k) p", p=P)).then_inc(gains_landed, 16)
            sp.dma_start(gain_nat[:, 1, :], pool_scale.rearrange("o (k p) -> (o k) p", p=P)).then_inc(gains_landed, 16)
            sp.dma_start(gain_nat[:, 2, :], g_ffn_pre.rearrange("o (k p) -> (o k) p", p=P)).then_inc(gains_landed, 16)
            for n in range(2):
                load(U_F + n, 0, win(8 * n, 8, OFF_F, P), 8, P)
            for s, g in enumerate(ORDER):
                for n in range(4):
                    load(U_U + 4 * s + n, 0, win(4 * n, 4, OFF_U + 256 * g, 256), 4, 256)
            for s, g in enumerate(ORDER):
                load(U_POOL + s, 0, wpool_v[g], 2, 512)

            def head_pair(n, more, hp):
                for part in range(3):
                    for half in range(2):
                        load(n + 2 * part + half, more, win(8 * half, 8, hp * P + part * AW, P), 8, P)

            for hp in range(2):
                head_pair(U_HP + 6 * hp, 0, hp)
            with sp.Fori(0, 3) as i:
                for j in range(2):
                    head_pair(U_HP + 12 + 6 * j, i * 12, i * 2 + (2 + j))

            def gate_pair(n, more, jp):
                for q in range(4):
                    load(n + q, more, win(4 * q, 4, jp * 256 + OFF_GA, 256), 4, 256)
                for q in range(4):
                    load(n + 4 + q, more, win(4 * q, 4, jp * 256 + OFF_GB, 256), 4, 256)
                for q in range(2):
                    load(n + 8 + q, more, wup_v[:, 4 * q:4 * q + 4, bass.ds(jp * 256, 256)], 4, 256,
                         apart=q == 0)

            for jp in range(2):
                gate_pair(U_GATE + 10 * jp, 0, jp)
            with sp.Fori(0, 3) as i:
                for j in range(2):
                    gate_pair(U_GATE + 20 + 10 * j, i * 20, i * 2 + (2 + j))
            with sp.Fori(0, 2) as i:
                for j in range(2):
                    for q in range(8):
                        load(U_OUT + 8 * j + q, i * 16,
                             wout_v[:, 2 * q:2 * q + 2, bass.ds(i * 1024 + 512 * j, 512)], 2, 512)
            with sp.Fori(0, NCHUNK) as c:
                for pr in range(4):
                    for q in range(4):
                        load(U_FFN + 4 * pr + q, c * 32,
                             wff1_v[:, 4 * q:4 * q + 4, bass.ds(c * CHUNK + 256 * pr, 256)], 4, 256)
                for cg in range(4):
                    for q in range(4):
                        load(U_FFN + 16 + 4 * cg + q, c * 32,
                             wff2_v[:, bass.ds(c * 8 + 2 * q, 2), 512 * cg:512 * cg + 512], 2, 512)

            for t in range(TT):
                for half in range(2):
                    cols = slice(half * (D // 2), (half + 1) * (D // 2))
                    sp.wait_ge(out_ready, 2 * t + half + 1)
                    sp.dma_start(yp_v[:, t, cols] if t < 2 else ys_v[:, cols],
                                 z_gain[:, t, cols]).then_inc(stored, 16)
            sp.wait_ge(stored, 32 * TT)

        @block.tensor
        def _(pe):
            def unit(n, more):
                pe.wait_ge(lo_ready, n + 1 + more)
                return n % RING

            def across(n, more, bank, tiles, k0, nk, x_hi, x_lo, k_last, parts=(0, 1)):
                slot = unit(n, more)
                w = tiles * P
                wh = w_hi[:, slot, :].rearrange("p (k w) -> p k w", w=w)
                wl = w_lo[:, slot, :].rearrange("p (k w) -> p k w", w=w)
                last = None
                for k in range(nk // 2 * parts[0], nk // 2 * (parts[-1] + 1)):
                    for c in range(tiles):
                        out = ps[:, bank + c, 0:T]
                        cols = slice(c * P, (c + 1) * P)
                        kk = k0 + k
                        pe.matmul(out, wh[:, k, cols], x_hi[:, kk, :], start=(kk == 0), stop=False)
                        pe.matmul(out, wh[:, k, cols], x_lo[:, kk, :], start=False, stop=False)
                        last = pe.matmul(out, wl[:, k, cols], x_hi[:, kk, :], start=False,
                                         stop=(kk == k_last))
                if parts[-1] == 1:
                    last.then_inc(unit_used, 1)
                return last

            def down(n, more, banks, k0, x_hi, x_lo, k_last, ended, tiles=(0, 1, 2)):
                slot = unit(n, more)
                wh = w_hi[:, slot, :].rearrange("p (k w) -> p k w", w=512)
                wl = w_lo[:, slot, :].rearrange("p (k w) -> p k w", w=512)
                for t in tiles:
                    out = ps[:, banks[t], :]
                    rows = slice(t * P, (t + 1) * P)
                    for k in range(2):
                        kk = k0 + k
                        pe.matmul(out, x_hi[:, kk, rows], wh[:, k, :], start=(kk == 0), stop=False)
                        pe.matmul(out, x_hi[:, kk, rows], wl[:, k, :], start=False, stop=False)
                        last = pe.matmul(out, x_lo[:, kk, rows], wh[:, k, :], start=False,
                                         stop=(kk == k_last))
                    if t == TT - 1:
                        last.then_inc(unit_used, 1)
                    elif k0 + 1 == k_last:
                        last.then_inc(ended, 1)

            pe.wait_ge(pool_const, 1)
            pe.wait_ge(gains_landed, 48)
            for n in range(3):
                last = pe.transpose(ps[:, 0, n * KD:(n + 1) * KD], gain_nat[:, n, :], ident[0:KD, 0:KD])
            last.then_inc(gain_psum, 1)
            pe.wait_ge(xn_ready, TT)

            def turn_x(k):
                if k >= 6:
                    pe.wait_ge(ht_lo_ready, k - 5)
                for t in range(TT):
                    last = pe.transpose(ps[:, 2 + k % 6, t * P:(t + 1) * P],
                                        x_sb[:, t, k * P:(k + 1) * P], ident[:, :])
                last.then_inc(ht_psum, 1)

            for k in range(6):
                turn_x(k)
            for n in range(4):
                for k in range(6 + 4 * n, min(10 + 4 * n, KD)):
                    turn_x(k)
                pe.wait_ge(ht_lo_ready, 4 * n + 4)
                across(U_F + n // 2, 0, 0, 1, 8 * (n // 2), 8, ht_hi, ht_lo, KD - 1, (n % 2,))
            pe.wait_ge(state_landed, 16)
            for n in range(2):
                for c in range(4):
                    last = pe.transpose(ps[:, 6 + n, c * P:c * P + BD * HIST],
                                        st_nat[:, (4 * n + c) * P:(4 * n + c + 1) * P],
                                        ident[0:BD * HIST, 0:BD * HIST])
                last.then_inc(aux_psum, 1)
            pe.wait_ge(clf_landed, 32)
            for t in range(BATCH_KEYS):
                last = pe.transpose(ps[:, 2, t * P:(t + 1) * P], clf[:, t, :], ident[:, :])
            last.then_inc(aux_psum, 1)

            for s in range(GROUPS):
                if s == 1:
                    pe.wait_ge(hist_saved, 2)
                elif s >= 2:
                    pe.wait_ge(u_saved, 2 * (s - 1))
                for q in range(4):
                    across(U_U + 4 * s + q, 0, 4 + 2 * (s % 2), 2, 4 * q, 4, ht_hi, ht_lo, KD - 1)
                if s == 1:
                    pe.wait_ge(f_dve, 12)
                    for t in range(TT):
                        last = pe.transpose(ps[:, 3, t * H:(t + 1) * H], logf_t[:, t * P:(t + 1) * P],
                                            ident[0:H, 0:H])
                    last.then_inc(fnat_psum, 1)

            for s, g in enumerate(ORDER):
                pe.wait_ge(pl_lo_ready, s + 1)
                slot = unit(U_POOL + s, 0)
                wh = w_hi[:, slot, :].rearrange("p (k w) -> p k w", w=512)
                wl = w_lo[:, slot, :].rearrange("p (k w) -> p k w", w=512)
                for j in range(4):
                    if s == 0:
                        pe.wait_ge([f_dve, f_dve, aux_saved, fnat_saved][j], 1)
                    else:
                        pe.wait_ge([brb_act, brb_act, brb_dve, brb_dve][j], 2 * (s - 1) + 1 + j % 2)
                    for k in range(2):
                        cols = slice(j * P, (j + 1) * P)
                        kk = 2 * g + k
                        pe.matmul(ps[:, j, 0:T], wh[:, k, cols], pl_hi[:, kk, :], start=(k == 0), stop=False)
                        pe.matmul(ps[:, j, 0:T], wh[:, k, cols], pl_lo[:, kk, :], start=False, stop=False)
                        last = pe.matmul(ps[:, j, 0:T], wl[:, k, cols], pl_hi[:, kk, :], start=False,
                                         stop=(k == 1))
                    if j < 3:
                        last.then_inc(brb_psum, 1)
                last.then_inc(unit_used, 1)
                if s == 1:
                    pe.wait_ge(u_saved, 2 * GROUPS)
                    for n in range(2):
                        for c in range(4):
                            last = pe.transpose(ps[0:QS, 4 + n, c * P:(c + 1) * P],
                                                u_p[:, 4 * n + c, HIST + SEQ - QS:HIST + SEQ], ident[:, :])
                        last.then_inc(unat_psum, 1)
                    for n in range(2):
                        for c in range(4):
                            last = pe.transpose(ps[:, 6 + n, c * P:(c + 1) * P], u_new[:, 4 * n + c, :],
                                                ident[:, :])
                        last.then_inc(unat_psum, 1)

            def rows_back(a, par):
                pe.wait_ge(k_saved, a + 1)
                pe.wait_ge(v_saved, a + 1)
                for x, src in ((0, kt[par]), (1, vt)):
                    if later(a):
                        pe.wait_ge(tp_free[x], a * 5)
                    for t in range(TT):
                        last = pe.transpose(ps[:, TP[x], t * P:(t + 1) * P], src[:, t * P:(t + 1) * P],
                                            ident[:, :])
                    last.then_inc(tp_full[x], 1)

            def scores_prompt(a, par):
                pe.wait_ge(q_saved, a + 1)
                if later(a):
                    pe.wait_ge(a_lo_ready, a * 2)
                for h in range(2):
                    last = pe.matmul(ps[:, S[0], h * P:(h + 1) * P], qp[par][:, h, 0:P], kt[par][:, 0:P],
                                     start=True, stop=True)
                last.then_inc(s_full[0], 1)
                if later(a):
                    pe.wait_ge(onat_ready, a)
                for h in range(2):
                    last = pe.matmul(ps[:, S[1], h * SEQ:(h + 1) * SEQ], qp[par][:, h, P:SEQ],
                                     kt[par][:, 0:SEQ], start=True, stop=True)
                last.then_inc(s_full[1], 1)

            def cache_keys(a, half):
                if half == 0:
                    pe.wait_ge(kc_landed, a * 16 + 16)
                for x in range(2):
                    pe.wait_ge(tp_free[x], a * 5 + 1 + half)
                    for n in range(4):
                        tile = (4 * half + 2 * x) * BATCH_KEYS + n
                        last = pe.transpose(ps[:, TP[x], n * P:(n + 1) * P], kc[:, tile, :], ident[:, :])
                    last.then_inc(tp_full[x], 1)

            def scores_sample(a, par, half):
                bank = S[2 + half]
                if half == 0:
                    if later(a):
                        pe.wait_ge(a_lo_ready, a * 2)
                else:
                    if later(a):
                        pe.wait_ge(max_ready, a * 6)
                pe.wait_ge(tp_free[0], a * 5 + 2 + half)
                pe.wait_ge(tp_free[1], a * 5 + 2 + half)
                pe.matmul(ps[:, bank, PAST:SCOL],
                          qs[par][:, 4 * half:4 * half + 4, :, :].rearrange("p b h q -> p (b h q)"),
                          kt[par][:, SEQ:T], start=True, stop=True)
                for b in range(4):
                    last = pe.matmul(ps[32 * b:32 * b + 32, bank, 0:PAST],
                                     qs[par][:, 4 * half + b, :, :].rearrange("p h q -> p (h q)"),
                                     kts[:, b, :], start=True, stop=True, tile_position=(0, 32 * b))
                last.then_inc(s_full[2 + half], 1)

            def turn_prompt(a):
                pe.wait_ge(prob_ready, a + 1)
                for x in range(2):
                    pe.wait_ge(tp_free[x], a * 5 + 3)
                    for n in range(3):
                        last = pe.transpose(ps[:, TP[x], n * P:(n + 1) * P], s_p[:, x, n * P:(n + 1) * P],
                                            ident[:, :])
                    last.then_inc(tp_full[x], 1)

            def turn_sample(a):
                for x in range(2):
                    pe.wait_ge(exp_ready, a * 6 + 5 + x)
                    pe.wait_ge(tp_free[x], a * 5 + 4)
                    for n in range(3):
                        last = pe.transpose(ps[:, TP[x], n * P:(n + 1) * P], s_s[:, x, n * P:(n + 1) * P],
                                            ident[:, :])
                    last.then_inc(tp_full[x], 1)

            def mix_prompt(a):
                pe.wait_ge(tp_free[0], a * 5 + 4)
                pe.wait_ge(tp_free[1], a * 5 + 4)
                pe.wait_ge(max_ready, a * 6 + 2)
                for h in range(2):
                    rows = slice(HD * h, HD * (h + 1))
                    pe.matmul(ps[rows, S[0], 0:P], v_nat[:, 0, rows], pt_p[:, h, 0:P],
                              start=True, stop=True, tile_position=(0, HD * h))
                    pe.matmul(ps[rows, S[0], P:SEQ], v_nat[:, 0, rows], pt_p[:, h, P:SEQ],
                              start=True, stop=False, tile_position=(0, HD * h))
                    last = pe.matmul(ps[rows, S[0], P:SEQ], v_nat[:, 1, rows], pt_p[:, h, SEQ:SEQ + P],
                                     start=False, stop=True, tile_position=(0, HD * h))
                last.then_inc(s_full[0], 1)

            def mix_sample(a):
                pe.wait_ge(tp_free[0], a * 5 + 5)
                pe.wait_ge(tp_free[1], a * 5 + 5)
                pe.wait_ge(vc_landed, a * 16 + 16)
                pe.wait_ge(max_ready, a * 6 + 4)
                for half in range(2):
                    cols = slice(half * P, (half + 1) * P)
                    for b in range(4):
                        for t in range(BATCH_KEYS):
                            rows = slice(32 * b, 32 * b + 32)
                            pe.matmul(ps[rows, S[1], cols],
                                      pt_s[:, half, t * P + 32 * b:t * P + 32 * b + 32],
                                      vc[:, (4 * half + b) * BATCH_KEYS + t, :],
                                      start=(t == 0), stop=(t == BATCH_KEYS - 1), tile_position=(0, 32 * b))
                    last = pe.matmul(ps[:, S[1], cols], pt_s[:, half, PAST:SCOL], v_nat[:, 2, :],
                                     start=False, stop=True, skip_group_check=True)
                last.then_inc(s_full[1], 1)

            def turn_out(a):
                pe.wait_ge(onat_ready, a + 1)
                pe.wait_ge(max_ready, a * 6 + 5)
                for half in range(2):
                    last = pe.transpose(ps[:, S[2], half * P:(half + 1) * P], o_nat[:, half, :], ident[:, :])
                last.then_inc(s_full[2], 1)

            def proj(n, more, hp, half, which, parts=(0, 1)):
                if half == 0 and parts[0] == 0:
                    if which == 0 and later(hp):
                        pe.wait_ge(k_saved, hp)
                    if which == 1 and later(hp):
                        pe.wait_ge(v_saved, hp)
                    if which == 2:
                        pe.wait_ge(q_saved, hp + 1)
                bank = G[(par_of[0] + which) % 2]
                across(n, more, bank, 1, 8 * half, 8, ht_hi, ht_lo, KD - 1, parts)

            par_of = [0]

            def head_pair(n, more, hp, par, attend):
                par_of[0] = par
                a, pa = hp - 1, 1 - par
                proj(n, more, hp, 0, 0)
                if attend:
                    rows_back(a, pa)
                    scores_prompt(a, pa)
                proj(n + 1, more, hp, 1, 0)
                if attend:
                    cache_keys(a, 0)
                proj(n + 2, more, hp, 0, 1)
                if attend:
                    scores_sample(a, pa, 0)
                    cache_keys(a, 1)
                proj(n + 3, more, hp, 1, 1)
                if attend:
                    scores_sample(a, pa, 1)
                    turn_prompt(a)
                proj(n + 4, more, hp, 0, 2)
                if attend:
                    turn_sample(a)
                    mix_prompt(a)
                proj(n + 5, more, hp, 1, 2, (0,))
                if attend:
                    mix_sample(a)
                proj(n + 5, more, hp, 1, 2, (1,))
                if attend:
                    turn_out(a)

            pe.wait_ge(brb_act, 2 * GROUPS)
            pe.wait_ge(brb_dve, 2 * GROUPS)
            pe.wait_ge(unat_saved, 4)
            head_pair(U_HP, 0, 0, 0, False)
            head_pair(U_HP + 6, 0, 1, 1, True)
            with pe.Fori(0, 3) as i:
                for j in range(2):
                    head_pair(U_HP + 12 + 6 * j, i * 12, i * 2 + (2 + j), j, True)

            def gate_a(n, more, q):
                return across(n + q, more, 0, 2, 4 * q, 4, ht_hi, ht_lo, KD - 1)

            def gate_b(n, more, jp):
                for q in range(4):
                    across(n + 4 + q, more, 2, 2, 4 * q, 4, ht_hi, ht_lo, KD - 1)

            def branch_a(n, more, jp):
                for q in range(2):
                    across(n + 8 + q, more, 4, 2, 4 * q, 4, at_hi, at_lo, PAIRS - 1)

            def gate_pair(n, more, jp):
                pe.wait_ge(ga_ready, jp)
                for q in range(4):
                    gate_a(n, more, q)
                pe.wait_ge(gb_ready, jp)
                gate_b(n, more, jp)
                pe.wait_ge(ta_ready, jp)
                branch_a(n, more, jp)

            pe.wait_ge(q_saved, 8)
            pe.wait_ge(k_saved, 8)
            pe.wait_ge(v_saved, 8)
            gate_a(U_GATE, 0, 0)
            rows_back(7, 1)
            scores_prompt(7, 1)
            gate_a(U_GATE, 0, 1)
            cache_keys(7, 0)
            gate_a(U_GATE, 0, 2)
            scores_sample(7, 1, 0)
            cache_keys(7, 1)
            gate_a(U_GATE, 0, 3)
            scores_sample(7, 1, 1)
            turn_prompt(7)
            turn_sample(7)
            mix_prompt(7)
            mix_sample(7)
            turn_out(7)
            pe.wait_ge(tp_free[0], 8 * 5)
            pe.wait_ge(tp_free[1], 8 * 5)
            gate_b(U_GATE, 0, 0)
            pe.wait_ge(a_lo_ready, 16)
            branch_a(U_GATE, 0, 0)
            gate_pair(U_GATE + 10, 0, 1)
            with pe.Fori(0, 3) as i:
                for j in range(2):
                    gate_pair(U_GATE + 20 + 10 * j, i * 20, i * 2 + (2 + j))

            pe.wait_ge(ga_ready, KD // 2)
            pe.wait_ge(gb_ready, KD // 2)
            for i in range(2):
                for j in range(2):
                    if later(i):
                        pe.wait_ge(ssq_ready[1], i * 6 - 2 + 3 * j)
                    for q in range(8):
                        if i + j == 0:
                            pe.wait_ge(m_lo_ready, q + 1)
                        down(U_OUT + 8 * j + q, i * 16, [3 * j, 3 * j + 1, 3 * j + 2], 2 * q,
                             mt_hi, mt_lo, KD - 1, y_psum)

            def turn_h(k, tiles):
                if k >= 6:
                    pe.wait_ge(h2_lo_ready, k - 5)
                for t in tiles:
                    last = pe.transpose(ps[:, [4, 5, 6, 7, 0, 1][k % 6], t * P:(t + 1) * P],
                                        ybuf[:, t, k * P:(k + 1) * P], ident[:, :])
                if tiles[-1] == TT - 1:
                    last.then_inc(h2_psum, 1)

            pe.wait_ge(hn_ready, 1)
            pe.wait_ge(hn1_ready, 1)
            for k in range(6):
                turn_h(k, (0, 1))
            pe.wait_ge(hn_ready, 2)
            for k in range(6):
                turn_h(k, (2,))

            def chunk(c, is_last=False):
                for pr in range(4):
                    if pr == 1 and later(c):
                        pe.wait_ge(o_added, c * 12)
                    elif pr >= 2:
                        pe.wait_ge(relu_ready, c * 4 + (pr - 1))
                    elif pr == 0 and later(c):
                        pe.wait_ge(relu_ready, c * 4)
                    for q in range(4):
                        if pr == 0 and not later(c):
                            for k in range(6 + 4 * q, min(10 + 4 * q, KD)):
                                turn_h(k, (0, 1, 2))
                            pe.wait_ge(h2_lo_ready, 4 * q + 4)
                        across(U_FFN + 4 * pr + q, c * 32, 2 - 2 * (pr % 2), 2, 4 * q, 4,
                               ht_hi, ht_lo, KD - 1)
                for cg in range(4):
                    banks = [[4, 5, 6], [7, 0, 1]][cg % 2]
                    if cg == 0 and later(c):
                        pe.wait_ge(o_added, c * 12)
                    elif cg == 1:
                        pe.wait_ge(relu_ready, c * 4 + 4)
                    elif cg >= 2:
                        pe.wait_ge(o_added, c * 12 + 3 * (cg - 1))
                    for tiles in ((0,), (1,), (2,)) if is_last and cg == 3 else ((0, 1, 2),):
                        for q in range(4):
                            if cg == 0:
                                pe.wait_ge(z_lo_ready, c * 4 + (q + 1))
                            down(U_FFN + 16 + 4 * cg + q, c * 32, banks, 2 * q, z_hi, z_lo,
                                 CHUNK // P - 1, o_psum, tiles)

            chunk(0)
            with pe.Fori(1, NCHUNK - 1) as c:
                chunk(c)
            chunk(NCHUNK - 1, True)

        @block.scalar
        def _(act):
            def slot(n, more):
                u = n + AHEAD
                if u >= UNITS:
                    return
                act.wait_ge(raw_landed[u % RING], (u // RING + 1) * 16 + more * 4)
                if u >= RING:
                    act.wait_ge(unit_used, u - RING + 1 + more)
                nc.scalar.copy(w_hi[:, u % RING, :], w_raw[:, u % RING, :]).then_inc(hi_ready, 1)

            for t in range(TT):
                act.wait_ge(x_landed[t], 16)
                nc.scalar.activation(junk0[:, :], x_sb[:, t, :], ACT.Square,
                                     accum_out=ssq[:, 0, t, 0:1]).then_inc(ssq_ready[0], 1)
                act.wait_ge(var_ready[0], t + 1)
                nc.scalar.activation(std[:, 0, t:t + 1], var[:, 0, t:t + 1], ACT.Sqrt).then_inc(std_ready[0], 1)
            slot(-2, 0)
            slot(-1, 0)
            act.wait_ge(gain_ready, 1)
            for k in range(KD):
                act.wait_ge(ht_psum, k + 1)
                nc.scalar.activation(ht_hi[:, k, :], ps[:, 2 + k % 6, 0:T], ACT.Copy,
                                     scale=g_pre_t[:, k:k + 1]).then_inc(ht_hi_ready, 1)

            slot(U_F, 0)
            slot(U_F + 1, 0)
            slot(U_U, 0)
            act.wait_ge(f_dve, 3)
            nc.scalar.activation(f_exp[:, :], f_abs[:, :], ACT.Exp, scale=-1.0).then_inc(f_act, 1)
            act.wait_ge(f_dve, 4)
            nc.scalar.activation(f_log[:, :], f_one[:, :], ACT.Ln).then_inc(f_act, 1)
            slot(U_U + 1, 0)
            for n in range(2):
                act.wait_ge(aux_psum, n + 1)
                src = ps[:, 6 + n, :].rearrange("p (c x) -> p c x", c=4)[:, :, 0:BD * HIST]
                for c in range(4):
                    last = nc.scalar.copy(u_s[:, 4 * n + c, :, 0:HIST],
                                                 src[:, c, :].rearrange("p (b j) -> p b j", j=HIST))
                last.then_inc(hist_saved, 1)

            def pool_hi(s, g):
                act.wait_ge(pooled_ready, s + 1)
                nc.scalar.copy(pl_hi[:, 2 * g:2 * g + 2, :], pooled[:, :, :]).then_inc(pl_hi_ready, 1)

            for s, g in enumerate(ORDER):
                for q in range(4):
                    if s > 0 or q > 1:
                        slot(U_U + 4 * s + q, 0)
                    if q == 2 and s >= 1:
                        pool_hi(s - 1, ORDER[s - 1])
                act.wait_ge(unit_used, U_U + 4 * s + 4)
                b = 4 + 2 * (s % 2)
                nc.scalar.copy(u_p[:, 2 * g:2 * g + 2, HIST:HIST + SEQ], ps[:, b:b + 2, 0:SEQ]).then_inc(u_saved, 1)
                nc.scalar.copy(u_new[:, 2 * g:2 * g + 2, :], ps[:, b:b + 2, SEQ:T])
                for c in range(2):
                    last = nc.scalar.copy(u_s[:, 2 * g + c, :, HIST:HIST + QS],
                                          ps[:, b + c, SEQ:T].rearrange("p (b q) -> p b q", q=QS))
                last.then_inc(u_saved, 1)
            for s, g in enumerate(ORDER):
                slot(U_POOL + s, 0)
                if s == 1:
                    pool_hi(GROUPS - 1, ORDER[-1])
                for j in range(2):
                    act.wait_ge(brb_psum, 3 * s + j + 1)
                    nc.scalar.activation(brb[:, 4 * g + j, :], ps[:, j, 0:T], ACT.Copy,
                                         scale=pscale_t[:, 4 * g + j:4 * g + j + 1]).then_inc(brb_act, 1)

            def values_back(a):
                act.wait_ge(tp_full[1], a * 5 + 1)
                if later(a):
                    act.wait_ge(v_stored, a * 32)
                nc.scalar.copy(v_nat[:, :, :].rearrange("p t c -> p (t c)"),
                               ps[:, TP[1], 0:T]).then_inc(tp_free[1], 1)

            def exp_prompt(a):
                act.wait_ge(nmx_ready, a * 3 + 1)
                for qt, c0, c1 in ((0, 0, P), (1, P, P + SEQ)):
                    for h in range(2):
                        e = 2 * qt + h
                        nc.scalar.activation(s_p[:, h, c0:c1], s_p[:, h, c0:c1], ACT.Exp,
                                             bias=nmx[:, e:e + 1],
                                             accum_out=esum[:, e:e + 1]).then_inc(exp_ready, 1)

            def exp_sample(a, half):
                act.wait_ge(nmx_ready, a * 3 + 2 + half)
                e = 4 + half
                nc.scalar.activation(s_s[:, half, :], s_s[:, half, :], ACT.Exp, bias=nmx[:, e:e + 1],
                                     accum_out=esum[:, e:e + 1]).then_inc(exp_ready, 1)

            def keys_in(a, half):
                act.wait_ge(tp_full[1], a * 5 + 2 + half)
                nc.scalar.copy(kts[:, 2:4, :].rearrange("p b s -> p (b s)"),
                               ps[:, TP[1], :]).then_inc(tp_free[1], 1)

            def turned_prompt(a):
                act.wait_ge(tp_full[1], a * 5 + 4)
                nc.scalar.copy(pt_p[:, 1, :], ps[:, TP[1], 0:P + SEQ]).then_inc(tp_free[1], 1)

            def turned_sample(a):
                act.wait_ge(tp_full[1], a * 5 + 5)
                nc.scalar.copy(pt_s[:, 1, :], ps[:, TP[1], 0:SCOL]).then_inc(tp_free[1], 1)

            def out_prompt(a):
                act.wait_ge(s_full[0], a * 2 + 2)
                nc.scalar.copy(at_hi[:, bass.ds(a, 1), 0:SEQ], ps[:, S[0]:S[0] + 1, 0:SEQ]).then_inc(a_hi_ready, 1)

            def out_rows(a):
                act.wait_ge(s_full[1], a * 2 + 2)
                act.wait_ge(srec_ready, a + 1)
                for half in range(2):
                    last = nc.scalar.activation(o_nat[:, half, :], ps[:, S[1], half * P:(half + 1) * P],
                                                ACT.Copy, scale=erec[:, 4 + half:5 + half])
                last.then_inc(onat_ready, 1)

            def out_sample(a):
                act.wait_ge(s_full[2], a * 2 + 2)
                for h in range(2):
                    rows = slice(HD * h, HD * (h + 1))
                    src = ps[rows, S[2], 0:2 * P].rearrange("p (b h q) -> p b h q", h=2, q=QS)[:, :, h, :]
                    dst = at_hi[rows, bass.ds(a, 1), SEQ:T].rearrange("p o (b q) -> p (o b) q", q=QS)
                    last = nc.scalar.copy(dst, src)
                last.then_inc(a_hi_ready, 1)

            def queries(hp, par):
                act.wait_ge(unit_used, hp * 6 + (U_HP + 2))
                act.wait_ge(q_zero, 1)
                bank = G[par]
                for h in range(2):
                    rows = slice(HD * h, HD * (h + 1))
                    nc.scalar.mul(qp[par][rows, h, :], ps[rows, bank, 0:SEQ], SCALE)
                    last = nc.scalar.mul(qs[par][rows, :, h, :],
                                         ps[rows, bank, SEQ:T].rearrange("p (b q) -> p b q", q=QS), SCALE)
                last.then_inc(q_saved, 1)

            def values(hp, par):
                act.wait_ge(unit_used, hp * 6 + (U_HP + 6))
                nc.scalar.copy(vt[:, :], ps[:, G[par], 0:T]).then_inc(v_saved, 1)

            def head_pair(n, more, hp, par, attend):
                a = hp - 1
                slot(n, more)
                if attend:
                    values_back(a)
                    exp_prompt(a)
                slot(n + 1, more)
                queries(hp, par)
                if attend:
                    keys_in(a, 0)
                slot(n + 2, more)
                if attend:
                    exp_sample(a, 0)
                    keys_in(a, 1)
                slot(n + 3, more)
                if attend:
                    exp_sample(a, 1)
                    turned_prompt(a)
                slot(n + 4, more)
                if attend:
                    turned_sample(a)
                slot(n + 5, more)
                if attend:
                    out_prompt(a)
                    out_rows(a)
                values(hp, par)
                if attend:
                    out_sample(a)

            head_pair(U_HP, 0, 0, 0, False)
            act.wait_ge(pool_stored, 144)
            act.wait_ge(nc_stored, 144)
            head_pair(U_HP + 6, 0, 1, 1, True)
            with act.Fori(0, 3) as i:
                for j in range(2):
                    head_pair(U_HP + 12 + 6 * j, i * 12, i * 2 + (2 + j), j, True)

            def sigmoid_a(jp):
                act.wait_ge(unit_used, jp * 10 + (U_GATE + 4))
                if later(jp):
                    act.wait_ge(m_lo_ready, jp)
                nc.scalar.activation(sg_a[:, :, :], ps[:, 0:2, 0:T], ACT.Sigmoid).then_inc(ga_ready, 1)

            def sigmoid_b(jp):
                act.wait_ge(unit_used, jp * 10 + (U_GATE + 8))
                nc.scalar.activation(sg_b[:, :, :], ps[:, 2:4, 0:T], ACT.Sigmoid).then_inc(gb_ready, 1)

            def merged_hi(jp):
                act.wait_ge(m_ready, jp + 1)
                nc.scalar.copy(mt_hi[:, bass.ds(jp * 2, 2), :], sg_a[:, :, :]).then_inc(m_hi_ready, 1)

            def gate_pair(n, more, jp):
                slot(n, more)
                slot(n + 1, more)
                merged_hi(jp - 1)
                slot(n + 2, more)
                slot(n + 3, more)
                sigmoid_a(jp)
                for q in range(4, 8):
                    slot(n + q, more)
                sigmoid_b(jp)
                slot(n + 8, more)
                slot(n + 9, more)

            slot(U_GATE, 0)
            values_back(7)
            exp_prompt(7)
            slot(U_GATE + 1, 0)
            keys_in(7, 0)
            slot(U_GATE + 2, 0)
            exp_sample(7, 0)
            keys_in(7, 1)
            slot(U_GATE + 3, 0)
            exp_sample(7, 1)
            turned_prompt(7)
            turned_sample(7)
            out_prompt(7)
            out_rows(7)
            out_sample(7)
            sigmoid_a(0)
            for q in range(4, 8):
                slot(U_GATE + q, 0)
            sigmoid_b(0)
            slot(U_GATE + 8, 0)
            slot(U_GATE + 9, 0)
            act.wait_ge(k_stored, 256)
            act.wait_ge(v_stored, 256)
            gate_pair(U_GATE + 10, 0, 1)
            with act.Fori(0, 3) as i:
                for j in range(2):
                    gate_pair(U_GATE + 20 + 10 * j, i * 20, i * 2 + (2 + j))
            merged_hi(7)

            act.sem_inc(ssq_ready[1], 1)
            nc.scalar.activation(root_warm[:, :], var[:, 0, :], ACT.Sqrt)
            with act.Fori(0, 2) as i:
                for j in range(2):
                    for q in range(8):
                        slot(U_OUT + 8 * j + q, i * 16)
                    for t in range(TT):
                        act.wait_ge(y_saved, i * 6 + (3 * j + t + 1))
                        act.wait_ge(ssq_ready[1], i * 6 + (3 * j + t + 1))
                        nc.scalar.activation(
                            junk[:, :], ps[:, 3 * j + t, :], ACT.Square,
                            accum_out=ssq[:, 1, t, bass.ds(i * 2 + j, 1)]).then_inc(ssq_ready[1], 1)

            def root(m, t):
                act.wait_ge(var_ready[m], t + 1)
                nc.scalar.activation(std[:, m, t:t + 1], var[:, m, t:t + 1], ACT.Sqrt).then_inc(std_ready[m], 1)

            act.wait_ge(var_ready[1], 1)
            nc.scalar.activation(std[:, 1, :], var[:, 1, :], ACT.Sqrt).then_inc(std_ready[1], 1)

            for t in range(TT):
                for half in range(2):
                    use = 2 * t + half
                    cols = slice(half * (D // 2), (half + 1) * (D // 2))
                    act.wait_ge(x2_ready, use + 1)
                    if use > 0:
                        act.wait_ge(ssq_ready[2], use)
                    nc.scalar.activation(junk2[:, :], xres[:, t, cols], ACT.Square,
                                         accum_out=ssq[:, 2, t, half:half + 1]).then_inc(ssq_ready[2], 1)
                    if use == 4:
                        act.wait_ge(var_ready[2], 1)
                        nc.scalar.activation(std[:, 2, 0:2], var[:, 2, 0:2], ACT.Sqrt).then_inc(std_ready[2], 1)
            act.wait_ge(var_ready[2], 2)
            nc.scalar.activation(std[:, 2, 2:3], var[:, 2, 2:3], ACT.Sqrt).then_inc(std_ready[2], 1)
            nc.scalar.activation(ybuf[:, 1, :], xres[:, 1, :], ACT.Copy, scale=rstd[:, 2, 1:2]).then_inc(hn1_ready, 1)
            for k in range(KD):
                act.wait_ge(h2_psum, k + 1)
                nc.scalar.activation(ht_hi[:, k, :], ps[:, [4, 5, 6, 7, 0, 1][k % 6], 0:T], ACT.Copy,
                                     scale=g_fpre_t[:, k:k + 1]).then_inc(h2_hi_ready, 1)
                if k % 4 == 3 and k < KD - 1:
                    slot(U_FFN + k // 4, 0)

            def chunk(n, more, c, is_last=False):
                for pr in range(4):
                    for q in range(4):
                        if pr > 0 or q == 3 or later(c):
                            slot(n + 4 * pr + q, more)
                    act.wait_ge(unit_used, c * 32 + (U_FFN + 4 * pr + 4))
                    if pr > 0 or later(c):
                        act.wait_ge(sq_ready, c * 4 + pr)
                    b = 2 - 2 * (pr % 2)
                    nc.scalar.activation(z_relu[:, :, :], ps[:, b:b + 2, 0:T], ACT.Relu).then_inc(relu_ready, 1)
                    act.wait_ge(sq_ready, c * 4 + (pr + 1))
                    nc.scalar.copy(z_hi[:, 2 * pr:2 * pr + 2, :], z_sq[:, :, :]).then_inc(z_hi_ready, 1)
                for cg in range(4):
                    for q in range(4):
                        slot(n + 16 + 4 * cg + q, more)
                    if is_last:
                        for t in range(TT):
                            use = cg * TT + t
                            act.wait_ge(o_added, c * 12 + use + 1)
                            if use > 0:
                                act.wait_ge(ssq_ready[3], use)
                            nc.scalar.activation(junk3[:, :], ybuf[:, t, 512 * cg:512 * cg + 512], ACT.Square,
                                                 accum_out=ssq[:, 3, t, cg:cg + 1]).then_inc(ssq_ready[3], 1)
                            if cg == 3:
                                root(3, t)

            chunk(U_FFN, 0, 0)
            with act.Fori(1, NCHUNK - 1) as c:
                chunk(U_FFN, c * 32, c)
            chunk(U_FFN + 32 * (NCHUNK - 1), 0, NCHUNK - 1, True)

        @block.vector
        def _(dve):
            def slot(n, more):
                u = n + AHEAD
                if u >= UNITS:
                    return
                dve.wait_ge(hi_ready, u + 1 + more)
                nc.vector.tensor_tensor(w_lo[:, u % RING, :], w_raw[:, u % RING, :],
                                        f32(w_hi[:, u % RING, :]), ALU.subtract).then_inc(lo_ready, 1)

            norm_steps = [0]

            def norm_step(ins):
                norm_steps[0] += 1
                ins.then_inc(norm_done, 1)
                dve.wait_ge(norm_done, norm_steps[0])

            def norm_var(m, t0, t1, parts=1):
                total = ssq[:, m, t0:t1, 0]
                if parts > 1:
                    total = ssq_sum[:, m, t0:t1]
                    norm_step(nc.vector.tensor_reduce(total, ssq[:, m, t0:t1, 0:parts],
                                                      mybir.AxisListType.X, ALU.add))
                nc.vector.tensor_scalar(var[:, m, t0:t1], total, 1.0 / D, EPS,
                                        ALU.mult, ALU.add).then_inc(var_ready[m], 1)

            def norm_rstd(m, t0, t1, roots):
                dve.wait_ge(std_ready[m], roots)
                v, r, f = var[:, m, t0:t1], rstd[:, m, t0:t1], factor[:, m, t0:t1]
                norm_step(nc.vector.reciprocal(r, std[:, m, t0:t1]))
                if t1 - t0 == 1:
                    norm_step(nc.vector.scalar_tensor_tensor(out=f, in0=v, scalar=r, in1=r,
                                                             op0=ALU.mult, op1=ALU.mult))
                else:
                    norm_step(nc.vector.tensor_tensor(f, r, r, ALU.mult))
                    norm_step(nc.vector.tensor_tensor(f, f, v, ALU.mult))
                norm_step(nc.vector.tensor_scalar(f, f, -0.5, 1.5, ALU.mult, ALU.add))
                norm_step(nc.vector.tensor_tensor(r, r, f, ALU.mult))

            for t in range(TT):
                dve.wait_ge(ssq_ready[0], t + 1)
                norm_var(0, t, t + 1)
                norm_rstd(0, t, t + 1, t + 1)
                nc.vector.tensor_scalar(x_sb[:, t, :], x_sb[:, t, :], rstd[:, 0, t:t + 1], None,
                                        ALU.mult).then_inc(xn_ready, 1)
            dve.wait_ge(gain_psum, 1)
            nc.vector.tensor_copy(gains_t[:, :, :].rearrange("p n k -> p (n k)"),
                                  ps[:, 0, 0:3 * KD]).then_inc(gain_ready, 1)
            dve.wait_ge(gain_ready, 1)
            slot(-2, 0)
            slot(-1, 0)
            for k in range(KD):
                dve.wait_ge(ht_hi_ready, k + 1)
                nc.vector.scalar_tensor_tensor(out=ht_lo[:, k, :], in0=ps[:, 2 + k % 6, 0:T],
                                               scalar=g_pre_t[:, k:k + 1], in1=f32(ht_hi[:, k, :]),
                                               op0=ALU.mult, op1=ALU.subtract).then_inc(ht_lo_ready, 1)
            slot(U_F, 0)
            slot(U_F + 1, 0)
            nc.vector.memset(ones[:, :], 1.0).then_inc(dve_const, 1)
            dve.wait_ge(pool_const, 3)
            nc.vector.tensor_scalar(row_i[:, 1:2], row_i[:, 0:1], 5, 4, ALU.logical_shift_right,
                                    ALU.logical_shift_left).then_inc(dve_const, 1)
            nc.vector.tensor_scalar(row_i[:, 2:3], row_i[:, 0:1], 15, None, ALU.bitwise_and).then_inc(dve_const, 1)
            dve.wait_ge(dve_const, 3)
            nc.vector.tensor_copy(row_f[:, 0:2], row_i[:, 1:3]).then_inc(dve_const, 1)
            dve.wait_ge(dve_const, 4)
            nc.vector.tensor_scalar(col_f[:, :], col_f[:, :], row_f[:, 0:1], None, ALU.subtract).then_inc(dve_const, 1)
            dve.wait_ge(dve_const, 5)
            for half in range(2):
                off = 64.0 * half
                nc.vector.tensor_scalar(mask_t[:, half, :], col_f[:, :], off, row_f[:, 1:2],
                                        ALU.subtract, ALU.is_gt).then_inc(dve_const, 1)
                nc.vector.tensor_scalar(mask_new[:, half, :], col_f[:, :], off, 0.0,
                                        ALU.subtract, ALU.is_lt).then_inc(dve_const, 1)
            dve.wait_ge(dve_const, 9)
            nc.vector.tensor_tensor(mask_t[:, :, :], mask_t[:, :, :], mask_new[:, :, :], ALU.add).then_inc(dve_const, 1)
            dve.wait_ge(dve_const, 10)
            nc.vector.tensor_scalar(mask_new[:, :, :], mask_t[:, :, :], MASKED, None, ALU.mult).then_inc(dve_const, 1)
            for g in range(GROUPS):
                for c in range(2):
                    nc.vector.tensor_scalar(recip_cnt[:, g, c, :], cnt_f[:, :], float(2 << g), None,
                                            ALU.min).then_inc(dve_const, 1)
            dve.wait_ge(dve_const, 19)
            nc.vector.reciprocal(recip_cnt[:, :, :, :].rearrange("p g c t -> p (g c t)"),
                                 recip_cnt[:, :, :, :].rearrange("p g c t -> p (g c t)")).then_inc(dve_const, 1)

            dve.wait_ge(unit_used, U_F + 2)
            dve.wait_ge(bf_landed, 16)
            steps = [0]

            def f_step(ins):
                steps[0] += 1
                ins.then_inc(f_dve, 1)
                dve.wait_ge(f_dve, steps[0])

            f_step(nc.vector.tensor_scalar(f_x[:, :], ps[0:H, 0, 0:T], bf_t[:, 0:1], None, ALU.add))
            f_step(nc.vector.tensor_scalar(f_neg[:, :], f_x[:, :], 0.0, None, ALU.min))
            f_step(nc.vector.scalar_tensor_tensor(out=f_abs[:, :], in0=f_x[:, :], scalar=-1.0, in1=f_x[:, :],
                                                  op0=ALU.mult, op1=ALU.max))
            slot(U_U, 0)
            dve.wait_ge(f_act, 1)
            f_step(nc.vector.tensor_scalar(f_one[:, :], f_exp[:, :], 1.0, None, ALU.add))
            f_step(nc.vector.tensor_scalar(f_x[:, :], f_one[:, :], 1.0, None, ALU.subtract))
            f_step(nc.vector.tensor_scalar(f_abs[:, :], f_x[:, :], 1e-9, None, ALU.max))
            f_step(nc.vector.reciprocal(f_abs[:, :], f_abs[:, :]))
            slot(U_U + 1, 0)
            f_step(nc.vector.tensor_tensor(f_abs[:, :], f_abs[:, :], f_exp[:, :], ALU.mult))
            dve.wait_ge(f_act, 2)
            f_step(nc.vector.tensor_tensor(f_abs[:, :], f_abs[:, :], f_log[:, :], ALU.mult))
            f_step(nc.vector.scalar_tensor_tensor(out=f_log[:, :], in0=f_x[:, :], scalar=0.0, in1=f_exp[:, :],
                                                  op0=ALU.is_equal, op1=ALU.mult))
            f_step(nc.vector.tensor_tensor(f_abs[:, :], f_abs[:, :], f_log[:, :], ALU.add))
            f_step(nc.vector.tensor_tensor(logf_t[:, :], f_neg[:, :], f_abs[:, :], ALU.subtract))
            nc.vector.tensor_tensor_scan(ncp[:, :], ones[0:H, 0:SEQ], logf_t[:, 0:SEQ], 0.0,
                                         ALU.mult, ALU.subtract).then_inc(ncp_ready, 1)
            dve.wait_ge(aux_psum, 3)
            nc.vector.tensor_copy(logf_all[:, 0:PAST], ps[:, 2, 0:PAST]).then_inc(aux_saved, 1)

            def pool_lo(s, g):
                w = 2 << g
                fin = g % 2
                dve.wait_ge(win_level, sum(ORDER[n] + 1 for n in range(s + 1)))
                dve.wait_ge(u_saved, 2 * s + 2)
                if s >= 1:
                    dve.wait_ge(pl_hi_ready, s)
                    dve.wait_ge(pl_lo_ready, s)
                for c in range(2):
                    nc.vector.scalar_tensor_tensor(
                        out=pooled[:, c, HIST:SEQ], in0=win_p[:, fin, c, 2 * HIST:HIST + SEQ], scalar=1.0 / w,
                        in1=u_p[:, 2 * g + c, 2 * HIST:HIST + SEQ], op0=ALU.mult, op1=ALU.subtract)
                    nc.vector.scalar_tensor_tensor(
                        out=pooled[:, c, SEQ:T].rearrange("p (b q) -> p b q", q=QS),
                        in0=win_s[:, fin, c, :, HIST:HIST + QS], scalar=1.0 / w,
                        in1=u_s[:, 2 * g + c, :, HIST:HIST + QS], op0=ALU.mult, op1=ALU.subtract)
                nc.vector.tensor_tensor(first[:, g, :, :], win_p[:, fin, :, HIST:2 * HIST],
                                        recip_cnt[:, g, :, :], ALU.mult).then_inc(win_step, 1)
                dve.wait_ge(win_step, s + 1)
                nc.vector.tensor_tensor(pooled[:, :, 0:HIST], first[:, g, :, :],
                                        u_p[:, 2 * g:2 * g + 2, HIST:2 * HIST],
                                        ALU.subtract).then_inc(pooled_ready, 1)
                dve.wait_ge(pl_hi_ready, s + 1)
                nc.vector.tensor_tensor(pl_lo[:, 2 * g:2 * g + 2, :], pooled[:, :, :],
                                        f32(pl_hi[:, 2 * g:2 * g + 2, :]), ALU.subtract).then_inc(pl_lo_ready, 1)

            for s, g in enumerate(ORDER):
                for q in range(4):
                    if s > 0 or q > 1:
                        slot(U_U + 4 * s + q, 0)
                    if s == 1 and q == 1:
                        dve.wait_ge(logf_new_in, 128)
                        dve.wait_ge(aux_saved, 1)
                        nc.vector.tensor_tensor_scan(ncs[:, 0:PAST + QS], ones[:, :], logf_all[:, :], 0.0,
                                                     ALU.mult, ALU.subtract).then_inc(ncs_ready, 1)
                        dve.wait_ge(ncs_ready, 1)
                        for b in range(1, BD):
                            last = nc.vector.tensor_copy(ncs[:, PAST + QS * b:PAST + QS * (b + 1)],
                                                         ncs[:, PAST:PAST + QS])
                        last.then_inc(ncs_ready, 1)
                    if q == 2 and s >= 1:
                        pool_lo(s - 1, ORDER[s - 1])
                if s == 1:
                    dve.wait_ge(fnat_psum, 1)
                    nc.vector.tensor_copy(logf_nat[:, :, :].rearrange("p t h -> p (t h)"),
                                          ps[:, 3, 0:TT * H]).then_inc(fnat_saved, 1)
            for s, g in enumerate(ORDER):
                slot(U_POOL + s, 0)
                if s == 1:
                    pool_lo(GROUPS - 1, ORDER[-1])
                for j in range(2, 4):
                    if j == 2:
                        dve.wait_ge(brb_psum, 3 * s + 3)
                    else:
                        dve.wait_ge(unit_used, U_POOL + s + 1)
                    nc.vector.tensor_scalar(brb[:, 4 * g + j, :], ps[:, j, 0:T], pscale_t[:, 4 * g + j:4 * g + j + 1],
                                            None, ALU.mult).then_inc(brb_dve, 1)
                if s == 2:
                    for n in range(2):
                        dve.wait_ge(unat_psum, n + 1)
                        nc.vector.tensor_copy(un_p[:, 512 * n:512 * n + 512],
                                              ps[0:QS, 4 + n, :]).then_inc(unat_saved, 1)
                    for n in range(2):
                        dve.wait_ge(unat_psum, n + 3)
                        nc.vector.tensor_copy(u_nat[:, 512 * n:512 * n + 512], ps[:, 6 + n, :]).then_inc(unat_saved, 1)

            def keys_back(a):
                dve.wait_ge(tp_full[0], a * 5 + 1)
                if later(a):
                    dve.wait_ge(k_stored, a * 32)
                nc.vector.tensor_copy(k_nat[:, :, :].rearrange("p t c -> p (t c)"),
                                      ps[:, TP[0], 0:T]).then_inc(tp_free[0], 1)

            def biased(out, psum, bias, e):
                nc.vector.tensor_tensor_reduce(out, psum, bias, 1.0, LOWEST, ALU.add, ALU.max,
                                               mx[:, e:e + 1]).then_inc(max_ready, 1)

            def bias_prompt(a):
                for qt in range(2):
                    if qt == 0:
                        dve.wait_ge(bias_ready, a * 3 + 2)
                    dve.wait_ge(s_full[qt], a * 2 + 1)
                    dve.sem_inc(dve_waited, 1)
                    for h in range(2):
                        if qt == 0:
                            biased(s_p[:, h, 0:P], ps[:, S[0], h * P:(h + 1) * P], bias_0[:, h, :], h)
                        else:
                            biased(s_p[:, h, P:P + SEQ], ps[:, S[1], h * SEQ:(h + 1) * SEQ], bias_p[:, h, :],
                                   2 + h)
                dve.wait_ge(max_ready, a * 6 + 4)
                nc.vector.tensor_scalar(nmx[:, 0:4], mx[:, 0:4], -1.0, None, ALU.mult).then_inc(nmx_ready, 1)

            def bias_sample(a, half):
                if half == 0:
                    dve.wait_ge(bias_ready, a * 3 + 3)
                    dve.wait_ge(s_full[2], a * 2 + 1)
                else:
                    dve.wait_ge(s_full[3], a + 1)
                dve.sem_inc(dve_waited, 1)
                biased(s_s[:, half, :], ps[:, S[2 + half], 0:SCOL], bias_s[:, half, :], 4 + half)
                dve.wait_ge(max_ready, a * 6 + 5 + half)
                nc.vector.tensor_scalar(nmx[:, 4 + half:5 + half], mx[:, 4 + half:5 + half], -1.0, None,
                                        ALU.mult).then_inc(nmx_ready, 1)

            def keys_in(a, half):
                dve.wait_ge(tp_full[0], a * 5 + 2 + half)
                nc.vector.tensor_copy(kts[:, 0:2, :].rearrange("p b s -> p (b s)"),
                                      ps[:, TP[0], :]).then_inc(tp_free[0], 1)

            def normalise_prompt(a):
                dve.wait_ge(exp_ready, a * 6 + 4)
                nc.vector.reciprocal(erec[:, 0:4], esum[:, 0:4]).then_inc(erec_ready, 1)
                dve.wait_ge(erec_ready, a + 1)
                for e in range(4):
                    c = slice(0, P) if e < 2 else slice(P, P + SEQ)
                    last = nc.vector.tensor_scalar(s_p[:, e % 2, c], s_p[:, e % 2, c], erec[:, e:e + 1], None,
                                                   ALU.mult)
                last.then_inc(prob_ready, 1)

            def turned_prompt(a):
                dve.wait_ge(tp_full[0], a * 5 + 4)
                nc.vector.tensor_copy(pt_p[:, 0, :], ps[:, TP[0], 0:P + SEQ]).then_inc(tp_free[0], 1)

            def turned_sample(a):
                dve.wait_ge(tp_full[0], a * 5 + 5)
                nc.vector.tensor_copy(pt_s[:, 0, :], ps[:, TP[0], 0:SCOL]).then_inc(tp_free[0], 1)

            def recip_sample(a):
                dve.wait_ge(exp_ready, a * 6 + 6)
                nc.vector.reciprocal(erec[:, 4:6], esum[:, 4:6]).then_inc(srec_ready, 1)

            def out_prompt(a):
                dve.wait_ge(a_hi_ready, a * 2 + 1)
                nc.vector.tensor_tensor(at_lo[:, bass.ds(a, 1), 0:SEQ], ps[:, S[0]:S[0] + 1, 0:SEQ],
                                        f32(at_hi[:, bass.ds(a, 1), 0:SEQ]), ALU.subtract).then_inc(a_lo_ready, 1)

            def out_sample(a):
                dve.wait_ge(a_hi_ready, a * 2 + 2)
                for h in range(2):
                    rows = slice(HD * h, HD * (h + 1))
                    src = ps[rows, S[2], 0:2 * P].rearrange("p (b h q) -> p b h q", h=2, q=QS)[:, :, h, :]
                    hi = at_hi[rows, bass.ds(a, 1), SEQ:T].rearrange("p o (b q) -> p (o b) q", q=QS)
                    lo = at_lo[rows, bass.ds(a, 1), SEQ:T].rearrange("p o (b q) -> p (o b) q", q=QS)
                    last = nc.vector.tensor_tensor(lo, src, f32(hi), ALU.subtract)
                last.then_inc(a_lo_ready, 1)

            def keys(hp, par):
                dve.wait_ge(unit_used, hp * 6 + (U_HP + 4))
                dve.wait_ge(q_zero, 1)
                nc.vector.tensor_copy(kt[par][:, :], ps[:, G[1 - par], 0:T]).then_inc(k_saved, 1)

            def head_pair(n, more, hp, par, attend):
                a = hp - 1
                slot(n, more)
                if attend:
                    keys_back(a)
                    bias_prompt(a)
                slot(n + 1, more)
                if attend:
                    keys_in(a, 0)
                    normalise_prompt(a)
                slot(n + 2, more)
                if attend:
                    bias_sample(a, 0)
                    keys_in(a, 1)
                slot(n + 3, more)
                keys(hp, par)
                if attend:
                    bias_sample(a, 1)
                    turned_prompt(a)
                slot(n + 4, more)
                if attend:
                    recip_sample(a)
                    turned_sample(a)
                slot(n + 5, more)
                if attend:
                    out_prompt(a)
                    out_sample(a)

            head_pair(U_HP, 0, 0, 0, False)
            head_pair(U_HP + 6, 0, 1, 1, True)
            with dve.Fori(0, 3) as i:
                for j in range(2):
                    head_pair(U_HP + 12 + 6 * j, i * 12, i * 2 + (2 + j), j, True)

            def gated_a(jp):
                dve.wait_ge(unit_used, jp * 10 + (U_GATE + 10))
                dve.wait_ge(ga_ready, jp + 1)
                nc.vector.tensor_tensor(sg_a[:, :, :], ps[:, 4:6, 0:T], sg_a[:, :, :], ALU.mult).then_inc(ta_ready, 1)

            def merged_lo(jp):
                dve.wait_ge(m_hi_ready, jp + 1)
                nc.vector.tensor_tensor(mt_lo[:, bass.ds(jp * 2, 2), :], sg_a[:, :, :],
                                        f32(mt_hi[:, bass.ds(jp * 2, 2), :]), ALU.subtract).then_inc(m_lo_ready, 1)

            def gate_pair(n, more, jp):
                slot(n, more)
                slot(n + 1, more)
                merged_lo(jp - 1)
                for q in range(2, 10):
                    slot(n + q, more)
                gated_a(jp)

            slot(U_GATE, 0)
            keys_back(7)
            bias_prompt(7)
            slot(U_GATE + 1, 0)
            keys_in(7, 0)
            normalise_prompt(7)
            slot(U_GATE + 2, 0)
            bias_sample(7, 0)
            keys_in(7, 1)
            slot(U_GATE + 3, 0)
            bias_sample(7, 1)
            turned_prompt(7)
            recip_sample(7)
            turned_sample(7)
            out_prompt(7)
            out_sample(7)
            for q in range(4, 10):
                slot(U_GATE + q, 0)
            gated_a(0)
            gate_pair(U_GATE + 10, 0, 1)
            with dve.Fori(0, 3) as i:
                for j in range(2):
                    gate_pair(U_GATE + 20 + 10 * j, i * 20, i * 2 + (2 + j))
            merged_lo(7)

            with dve.Fori(0, 2) as i:
                for j in range(2):
                    for q in range(8):
                        slot(U_OUT + 8 * j + q, i * 16)
                    cols = bass.ds(i * 1024 + 512 * j, 512)
                    dve.wait_ge(gpost_landed, 16)
                    for t in range(TT):
                        if t < TT - 1:
                            dve.wait_ge(y_psum, i * 4 + (2 * j + t + 1))
                        else:
                            dve.wait_ge(unit_used, i * 16 + (U_OUT + 8 * j + 8))
                        nc.vector.tensor_tensor(ybuf[:, t, cols], ps[:, 3 * j + t, :], g_post_r[:, cols],
                                                ALU.mult).then_inc(y_saved, 1)

            dve.wait_ge(ssq_ready[1], 1 + 4 * TT)
            norm_var(1, 0, TT, 4)
            norm_rstd(1, 0, TT, 1)
            dve.wait_ge(xres_landed, 48)
            for t in range(TT):
                for half in range(2):
                    cols = slice(half * (D // 2), (half + 1) * (D // 2))
                    nc.vector.scalar_tensor_tensor(out=xres[:, t, cols], in0=ybuf[:, t, cols],
                                                   scalar=rstd[:, 1, t:t + 1], in1=xres[:, t, cols],
                                                   op0=ALU.mult, op1=ALU.add).then_inc(x2_ready, 1)
                    if t == 2 and half == 0:
                        dve.wait_ge(ssq_ready[2], 4)
                        norm_var(2, 0, 2, 2)

            def normed(t):
                nc.vector.tensor_scalar(ybuf[:, t, :], xres[:, t, :], rstd[:, 2, t:t + 1], None,
                                        ALU.mult).then_inc(hn_ready, 1)

            norm_rstd(2, 0, 2, 1)
            dve.wait_ge(ssq_ready[2], 6)
            norm_var(2, 2, 3, 2)
            normed(0)
            norm_rstd(2, 2, 3, 2)
            normed(2)
            for k in range(KD):
                dve.wait_ge(h2_hi_ready, k + 1)
                nc.vector.scalar_tensor_tensor(out=ht_lo[:, k, :], in0=ps[:, [4, 5, 6, 7, 0, 1][k % 6], 0:T],
                                               scalar=g_fpre_t[:, k:k + 1], in1=f32(ht_hi[:, k, :]),
                                               op0=ALU.mult, op1=ALU.subtract).then_inc(h2_lo_ready, 1)
                if k % 4 == 3 and k < KD - 1:
                    slot(U_FFN + k // 4, 0)

            def chunk(n, more, c, is_last=False):
                for pr in range(4):
                    for q in range(4):
                        if pr > 0 or q == 3 or later(c):
                            slot(n + 4 * pr + q, more)
                    dve.wait_ge(relu_ready, c * 4 + (pr + 1))
                    nc.vector.tensor_tensor(z_sq[:, :, :], z_relu[:, :, :], z_relu[:, :, :],
                                            ALU.mult).then_inc(sq_ready, 1)
                    dve.wait_ge(z_hi_ready, c * 4 + (pr + 1))
                    nc.vector.tensor_tensor(z_lo[:, 2 * pr:2 * pr + 2, :], z_sq[:, :, :],
                                            f32(z_hi[:, 2 * pr:2 * pr + 2, :]), ALU.subtract).then_inc(z_lo_ready, 1)
                if not later(c):
                    dve.wait_ge(acc_zero, 1)
                for cg in range(4):
                    for q in range(4):
                        slot(n + 16 + 4 * cg + q, more)
                    for t in range(TT):
                        if t < TT - 1:
                            dve.wait_ge(o_psum, c * 8 + (2 * cg + t + 1))
                        else:
                            dve.wait_ge(unit_used, c * 32 + (U_FFN + 16 + 4 * cg + 4))
                        bank = [[4, 5, 6], [7, 0, 1]][cg % 2][t]
                        cols = slice(512 * cg, 512 * cg + 512)
                        nc.vector.tensor_tensor(ybuf[:, t, cols], ps[:, bank, :], ybuf[:, t, cols],
                                                ALU.add).then_inc(o_added, 1)
                        if is_last:
                            if cg == 0 and t == 0:
                                dve.wait_ge(gfpost_landed, 16)
                            dve.wait_ge(o_added, c * 12 + 3 * cg + t + 1)
                            nc.vector.tensor_tensor(z_gain[:, t, cols], ybuf[:, t, cols], g_fpost_r[:, cols],
                                                    ALU.mult).then_inc(o_gained, 1)
                            if cg == 3:
                                finish(t)

            def finish(t):
                dve.wait_ge(ssq_ready[3], 3 * TT + t + 1)
                dve.wait_ge(o_gained, 3 * TT + t + 1)
                norm_var(3, t, t + 1, 4)
                norm_rstd(3, t, t + 1, t + 1)
                for half in range(2):
                    cols = slice(half * (D // 2), (half + 1) * (D // 2))
                    nc.vector.scalar_tensor_tensor(out=z_gain[:, t, cols], in0=z_gain[:, t, cols],
                                                   scalar=rstd[:, 3, t:t + 1], in1=xres[:, t, cols],
                                                   op0=ALU.mult, op1=ALU.add).then_inc(out_ready, 1)

            chunk(U_FFN, 0, 0)
            with dve.Fori(1, NCHUNK - 1) as c:
                chunk(U_FFN, c * 32, c)
            chunk(U_FFN + 32 * (NCHUNK - 1), 0, NCHUNK - 1, True)

        @block.gpsimd
        def _(pool):
            pool.dma_start(bf_t[:, :], b_f.rearrange("o h -> h o"),
                           allow_slow_non_contiguous=True).then_inc(bf_landed, 16)
            pool.dma_start(st_nat[:, :], state_pool.rearrange("o b j c -> (o b j) c")).then_inc(state_landed, 16)
            for t in range(BATCH_KEYS):
                pool.dma_start(clf[:, t, :].rearrange("p (b h) -> p b h", h=H), clf_v[t]).then_inc(clf_landed, 16)
            nc.gpsimd.memset(ident[:, :], 0.0).then_inc(ident_zero, 1)
            pool.wait_ge(ident_zero, 1)
            nc.gpsimd.affine_select(out=ident[:, :], in_=ident[:, :], compare_op=ALU.not_equal, fill=1.0, base=0,
                                    pattern=[[-1, P]], channel_multiplier=1).then_inc(pool_const, 1)
            nc.gpsimd.iota(row_i[:, 0:1], pattern=[[0, 1]], base=0, channel_multiplier=1).then_inc(pool_const, 1)
            nc.gpsimd.iota(cnt_f[:, :], pattern=[[1, HIST]], base=1, channel_multiplier=0,
                           allow_small_or_imprecise_dtypes=True)
            nc.gpsimd.iota(col_f[:, :], pattern=[[1, P]], base=0, channel_multiplier=0,
                           allow_small_or_imprecise_dtypes=True).then_inc(pool_const, 1)
            nc.gpsimd.memset(u_p[:, :, 0:HIST], 0.0).then_inc(pool_const, 1)

            pool.wait_ge(f_dve, 12)
            for b in range(BD):
                pool.dma_start(logf_all[H * b:H * (b + 1), PAST:PAST + QS],
                               logf_t[:, SEQ + QS * b:SEQ + QS * (b + 1)]).then_inc(logf_new_in, 16)
            pool.wait_ge(ncp_ready, 1)
            pool.dma_start(ncp_dram, ncp[:, :]).then_inc(nc_stored, 16)

            def windows(s, g):
                if s == 0:
                    pool.wait_ge(pool_const, 4)
                    pool.wait_ge(hist_saved, 2)
                pool.wait_ge(u_saved, 2 * s + 2)
                if s >= 1:
                    pool.wait_ge(pooled_ready, s)
                for lev in range(g + 1):
                    d, lo = 1 << lev, (2 << lev) - 1
                    src_p = u_p[:, 2 * g:2 * g + 2, :] if lev == 0 else win_p[:, (lev - 1) % 2, :, :]
                    if lev >= 1:
                        pool.wait_ge(win_level, levels[0])
                    dst = lev % 2
                    nc.gpsimd.tensor_tensor(win_p[:, dst, :, lo:], src_p[:, :, lo:],
                                            src_p[:, :, lo - d:HIST + SEQ - d], ALU.add)
                    for c in range(2):
                        src_s = u_s[:, 2 * g + c, :, :] if lev == 0 else win_s[:, (lev - 1) % 2, c, :, :]
                        last = nc.gpsimd.tensor_tensor(win_s[:, dst, c, :, lo:], src_s[:, :, lo:],
                                                       src_s[:, :, lo - d:HIST + QS - d], ALU.add)
                    levels[0] += 1
                    last.then_inc(win_level, 1)

            levels = [0]
            windows(0, ORDER[0])
            pool.wait_ge(ncs_ready, 2)
            for b in range(BD):
                pool.dma_start(ncs_dram[:, b, :, :],
                               ncs[H * b:H * (b + 1), :]).then_inc(nc_stored, 16)
            windows(1, ORDER[1])
            pool.wait_ge(fnat_saved, 1)
            pool.dma_start(lfp_v, logf_nat[:, 0:2, :]).then_inc(logf_stored, 16)
            pool.dma_start(lfs_v, logf_nat[:, 2, :]).then_inc(logf_stored, 16)
            windows(2, ORDER[2])
            windows(3, ORDER[3])
            pool.wait_ge(unat_saved, 4)
            pool.dma_start(pool_prompt[0, 0], un_p[1:QS, :]).then_inc(pool_stored, 16)
            for b in range(BD):
                pool.dma_start(pool_sample[0, b], u_nat[QS * b + 1:QS * (b + 1), :]).then_inc(pool_stored, 16)

            pool.wait_ge(unit_used, U_HP)
            pool.wait_ge(pool_stored, 144)
            for n in range(2):
                nc.gpsimd.memset(qp[n][:, :, :], 0.0)
                last = nc.gpsimd.memset(qs[n][:, :, :, :], 0.0)
            last.then_inc(q_zero, 1)
            pool.wait_ge(nc_stored, 144)
            pool.wait_ge(logf_stored, 32)

            def load_keys(a):
                pool.dma_start(kc[:, :, :], ck_v[:, :, bass.ds(a * P, P)]).then_inc(kc_landed, 16)

            def load_values(a):
                pool.dma_start(vc[:, :, :], cv_v[:, :, bass.ds(a * P, P)]).then_inc(vc_landed, 16)

            def load_bias(a):
                pool.dma_start(bias_p[:, :, :],
                               ncp_dram[bass.ds(a * 2, 2), :].unsqueeze(0).broadcast_to([P, 2, SEQ])
                               ).then_inc(bias_landed, 16)
                for half in range(2):
                    for b in range(4):
                        src = ncs_dram[bass.ds(a, 1), 4 * half + b, :, :]
                        src = src.rearrange("o h n -> h o n").broadcast_to([2, QS, SCOL])
                        pool.dma_start(bias_s[32 * b:32 * b + 32, half, :], src).then_inc(bias_landed, 16)
                pool.wait_ge(bias_landed, a * 144 + 144)
                pool.sem_inc(pool_waited, 1)
                nc.gpsimd.affine_select(out=bias_0[:, :, :], in_=bias_p[:, :, 0:P], compare_op=ALU.is_ge,
                                        fill=MASKED, base=0, pattern=[[0, 2], [-1, P]],
                                        channel_multiplier=1).then_inc(bias_ready, 1)
                nc.gpsimd.affine_select(out=bias_p[:, :, P:SEQ], in_=bias_p[:, :, P:SEQ], compare_op=ALU.is_ge,
                                        fill=MASKED, base=0, pattern=[[0, 2], [-1, P]],
                                        channel_multiplier=1).then_inc(bias_ready, 1)
                nc.gpsimd.tensor_tensor(bias_s[:, :, PAST:SCOL], bias_s[:, :, PAST:SCOL], mask_new[:, :, :],
                                        ALU.add).then_inc(bias_ready, 1)

            def store_rows(a):
                cols = bass.ds(a * P, P)
                pool.wait_ge(tp_free[0], a * 5 + 1)
                pool.sem_inc(pool_waited, 1)
                pool.dma_start(kp_v[:, :, cols], k_nat[:, 0:2, :]).then_inc(k_stored, 16)
                pool.dma_start(ks_v[:, cols], k_nat[:, 2, :]).then_inc(k_stored, 16)
                pool.wait_ge(tp_free[1], a * 5 + 1)
                pool.sem_inc(pool_waited, 1)
                pool.dma_start(vp_v[:, :, cols], v_nat[:, 0:2, :]).then_inc(v_stored, 16)
                pool.dma_start(vs_v[:, cols], v_nat[:, 2, :]).then_inc(v_stored, 16)

            pool.wait_ge(dve_const, 11)
            load_keys(0)
            load_bias(0)
            load_values(0)
            with pool.Fori(0, 7) as a:
                store_rows(a)
                pool.wait_ge(tp_full[0], a * 5 + 3)
                pool.wait_ge(tp_full[1], a * 5 + 3)
                load_keys(a + 1)
                pool.wait_ge(max_ready, a * 6 + 6)
                load_bias(a + 1)
                pool.wait_ge(s_full[1], a * 2 + 2)
                pool.sem_inc(pool_waited, 1)
                load_values(a + 1)
            store_rows(7)

            with pool.Fori(0, KD // 2) as jp:
                pool.wait_ge(gb_ready, jp + 1)
                nc.gpsimd.tensor_tensor(sg_b[:, :, :], sg_b[:, :, :], brb[:, bass.ds(jp * 2, 2), :],
                                        ALU.mult).then_inc(tb_ready, 1)
                pool.wait_ge(ta_ready, jp + 1)
                pool.wait_ge(tb_ready, jp + 1)
                nc.gpsimd.tensor_tensor(sg_a[:, :, :], sg_a[:, :, :], sg_b[:, :, :], ALU.add).then_inc(m_ready, 1)

            for t in range(TT):
                pool.dma_start(xres[:, t, :], xp_v[:, t, :] if t < 2 else xs_v).then_inc(xres_landed, 16)
            pool.wait_ge(m_lo_ready, KD // 2)
            pool.dma_start(g_post_r[:, :], g_mix_post.broadcast_to([P, D])).then_inc(gpost_landed, 16)
            pool.wait_ge(unit_used, U_OUT + 32)
            pool.dma_start(g_fpost_r[:, :], g_ffn_post.broadcast_to([P, D])).then_inc(gfpost_landed, 16)
            pool.wait_ge(h2_psum, KD)
            nc.gpsimd.memset(ybuf[:, :, :], 0.0).then_inc(acc_zero, 1)
            pool.wait_ge(k_stored, 256)
            pool.wait_ge(v_stored, 256)


_INS = ["x_prompt", "x_sample", "cache_k", "cache_v", "cache_logf", "state_pool", "g_mix_pre", "w_in",
        "b_f", "w_attn_up", "w_pool", "pool_scale", "w_out", "g_mix_post", "g_ffn_pre", "w_ff1", "w_ff2",
        "g_ffn_post"]
_OUTS = [(1, SEQ, D), (BD, QS, D), (1, 1, SEQ, H, HD), (1, 1, SEQ, H, HD), (1, 1, SEQ, H),
         (1, 1, HIST, POOLW), (1, BD, QS, H, HD), (1, BD, QS, H, HD), (1, BD, QS, H), (1, BD, HIST, POOLW)]


def kernel(**inputs):
    import numpy as _np
    import concourse.bacc as _bacc
    from concourse import mybir as _mybir
    from concourse.bass_utils import run_bass_kernel_spmd as _run

    nc = _bacc.Bacc("TRN2", target_bir_lowering=False, num_devices=1)
    arrays, args = {}, []
    for name in _INS:
        a = _np.ascontiguousarray(inputs[name])
        arrays[f"in_{name}_dram"] = a
        args.append(nc.dram_tensor(f"in_{name}_dram", a.shape, _mybir.dt.from_np(a.dtype),
                                   kind="ExternalInput").ap())
    for i, shape in enumerate(_OUTS):
        args.append(nc.dram_tensor(f"out_{i}_dram", shape, _mybir.dt.float32, kind="ExternalOutput").ap())
    streaming_encoder(nc, *args)
    r = _run(nc, [arrays], core_ids=[0])
    return tuple(r.results[0][f"out_{i}_dram"] for i in range(len(_OUTS)))
```
